# Optimizing a Trainium2 kernel written in Bass

```python
import jax, jax.numpy as jnp
from jax import lax
import numpy as np

D_MODEL = 1024
BATCH = 1
SEQ = 2048
DEPTH = 1
DEC_BATCH = 8
DEC_SEQ = 4
PAST_LEN = 16384
PAGE_SIZE = 128

D_MIX = D_MODEL
GROUP_W = D_MIX // 4
N_HEADS = 4
HEAD_K = GROUP_W // N_HEADS
HEAD_V = GROUP_W // N_HEADS
GLA_RANK = 16
GATE_NORM = 16.0
CONV_W = 3
POOL_WINDOWS = (2, 4, 8, 16)
POOL_GROUP = GROUP_W // len(POOL_WINDOWS)
POOL_BUF = max(POOL_WINDOWS) - 1
N_META = 16
CHUNK = 16
EPS = 1e-6

COLS = (('a_q', GROUP_W), ('a_k', GROUP_W), ('a_v', GROUP_W), ('a_lr', GLA_RANK), ('a_z', GROUP_W),
        ('b_b', GROUP_W), ('b_c', GROUP_W), ('b_v', GROUP_W), ('b_z', GROUP_W),
        ('c_q', GROUP_W), ('c_f', GROUP_W), ('c_i', GROUP_W), ('c_z', GROUP_W),
        ('d_v', GROUP_W), ('d_z', GROUP_W))
D_IN = sum(w for _, w in COLS)

kernel_name = 'hymba_gla_conv_hgrn2_pool_step'

F32 = jnp.float32

def _split_cols(p):
    out = {}
    off = 0
    for name, w in COLS:
        out[name] = p[..., off:off + w]
        off += w
    return out

def _rmsnorm(x, g):
    xf = x.astype(F32)
    y = xf * lax.rsqrt(jnp.mean(xf * xf, axis=-1, keepdims=True) + EPS)
    return (y * g.astype(F32)).astype(x.dtype)

def _head_rmsnorm(o, g):
    bsz, T, H, Dh = o.shape
    of = o.astype(F32)
    y = of * lax.rsqrt(jnp.mean(of * of, axis=-1, keepdims=True) + EPS)
    return (y.reshape(bsz, T, H * Dh) * g.astype(F32)).astype(o.dtype)

def _lower_bounds(gamma):
    p = jax.nn.softmax(gamma.astype(F32), axis=0)
    c = jnp.cumsum(p, axis=0)
    return c - c[0:1]

def _chunked_gated_linear(q, k, v, log_a, s0):
    bsz, T, H, DK = q.shape
    DV = v.shape[-1]
    C = min(CHUNK, T)
    n = -(-T // C)
    pad = n * C - T

    def blocks(a):
        a = jnp.pad(a.astype(F32), ((0, 0), (0, pad), (0, 0), (0, 0)))
        return a.reshape(bsz, n, C, H, a.shape[-1]).transpose(1, 0, 3, 2, 4)

    causal = jnp.tril(jnp.ones((C, C), dtype=bool))[None, None, :, :, None]

    def step(S, blk):
        qc, kc, vc, gc = blk
        b = jnp.cumsum(gc, axis=2)
        decay = jnp.exp(jnp.where(causal, b[:, :, :, None, :] - b[:, :, None, :, :], -jnp.inf))
        scores = jnp.einsum('bhtd,bhsd,bhtsd->bhts', qc, kc, decay)
        o = (jnp.einsum('bhts,bhsv->bhtv', scores, vc)
             + jnp.einsum('bhtd,bhdv->bhtv', qc * jnp.exp(b), S))
        b_last = b[:, :, -1, :]
        S = (jnp.exp(b_last)[..., None] * S
             + jnp.einsum('bhsd,bhsv->bhdv', kc * jnp.exp(b_last[:, :, None, :] - b), vc))
        return S, o

    S, o = lax.scan(step, s0.astype(F32), (blocks(q), blocks(k), blocks(v), blocks(log_a)))
    o = o.transpose(1, 0, 3, 2, 4).reshape(bsz, n * C, H, DV)[:, :T]
    return o.astype(v.dtype), S.astype(s0.dtype)

def _layer(x, l, s_gla, s_conv, s_hgrn, s_pool, pos0, lb,
           norm_pre, norm_post, w_in, gla_w_a2, gla_b_a, gla_norm, conv_w,
           hgrn_norm, pool_w, pool_scale, w_out):
    bsz, T, _ = x.shape
    dt = x.dtype
    h = _rmsnorm(x, norm_pre[l])
    c = _split_cols(h @ w_in[l])

    def heads(a):
        return a.reshape(bsz, T, N_HEADS, -1)

    q_a = c['a_q'] * HEAD_K ** -0.5
    log_a = jax.nn.log_sigmoid((c['a_lr'] @ gla_w_a2[l] + gla_b_a[l]).astype(F32)) / GATE_NORM
    o_a, s_gla_new = _chunked_gated_linear(heads(q_a), heads(c['a_k']), heads(c['a_v']), heads(log_a), s_gla)
    o_a = (_head_rmsnorm(o_a, gla_norm[l]) * jax.nn.silu(c['a_z'])).astype(dt)

    u_b = c['b_c'] * c['b_v']
    ext_b = jnp.concatenate([s_conv.astype(u_b.dtype), u_b], axis=1)
    conv = sum(ext_b[:, j:j + T] * conv_w[l, j] for j in range(CONV_W))
    o_b = (c['b_b'] * conv * jax.nn.silu(c['b_z'])).astype(dt)
    s_conv_new = ext_b[:, T:]

    fx = c['c_f'].astype(F32)
    lb_l = lb[l]
    log_f = jnp.logaddexp(jnp.log(lb_l), jnp.log1p(-lb_l) + jax.nn.log_sigmoid(fx))
    k_c = (1.0 - lb_l) * jax.nn.sigmoid(-fx)
    q_c = jax.nn.silu(c['c_q']) * HEAD_K ** -0.5
    o_c, s_hgrn_new = _chunked_gated_linear(heads(q_c), heads(k_c), heads(c['c_i']), heads(log_f), s_hgrn)
    o_c = (_head_rmsnorm(o_c, hgrn_norm[l]) * jax.nn.silu(c['c_z'])).astype(dt)

    u_d = c['d_v']
    ext_d = jnp.concatenate([s_pool.astype(u_d.dtype), u_d], axis=1)
    cs = jnp.pad(jnp.cumsum(ext_d.astype(F32), axis=1), ((0, 0), (1, 0), (0, 0)))
    pos = pos0 + jnp.arange(T)
    hi = POOL_BUF + 1
    groups = []
    for g, w in enumerate(POOL_WINDOWS):
        sl = slice(g * POOL_GROUP, (g + 1) * POOL_GROUP)
        win = cs[:, hi:hi + T, sl] - cs[:, hi - w:hi - w + T, sl]
        cnt = jnp.minimum(pos + 1, w).astype(F32)[None, :, None]
        groups.append(win / cnt - u_d[..., sl].astype(F32))
    pooled = jnp.stack(groups, axis=2)
    o_d = jnp.einsum('btgc,gcd->btgd', pooled, pool_w[l].astype(F32)).reshape(bsz, T, GROUP_W)
    o_d = (o_d * pool_scale[l] * jax.nn.silu(c['d_z'])).astype(dt)
    s_pool_new = ext_d[:, T:]

    mix = jnp.concatenate([o_a, o_b, o_c, o_d], axis=-1)
    x = x + _rmsnorm(mix @ w_out[l], norm_post[l])
    return x, s_gla_new, s_conv_new, s_hgrn_new, s_pool_new

def setup_inputs(seed: int = 0) -> dict:
    key = jax.random.key(seed)
    ks = jax.random.split(key, 19)

    def nrm(k, shape, scale):
        return jax.random.normal(k, shape, jnp.float32) * scale

    return {
        'x_prompt': nrm(ks[0], (BATCH, SEQ, D_MODEL), 1.0),
        'x_sample': nrm(ks[1], (DEC_BATCH, DEC_SEQ, D_MODEL), 1.0),
        'state_gla': nrm(ks[2], (DEPTH, DEC_BATCH, N_HEADS, HEAD_K, HEAD_V), 0.5),
        'state_conv': nrm(ks[3], (DEPTH, DEC_BATCH, CONV_W - 1, GROUP_W), 1.0),
        'state_hgrn': nrm(ks[4], (DEPTH, DEC_BATCH, N_HEADS, HEAD_K, HEAD_V), 0.5),
        'state_pool': nrm(ks[5], (DEPTH, DEC_BATCH, POOL_BUF, GROUP_W), 1.0),
        'meta_tokens': nrm(ks[6], (N_META, D_MODEL), 1.0),
        'norm_pre': 1.0 + nrm(ks[7], (DEPTH, D_MODEL), 0.1),
        'norm_post': 1.0 + nrm(ks[8], (DEPTH, D_MODEL), 0.1),
        'w_in': nrm(ks[9], (DEPTH, D_MODEL, D_IN), D_MODEL ** -0.5),
        'gla_w_a2': nrm(ks[10], (DEPTH, GLA_RANK, GROUP_W), GLA_RANK ** -0.5),
        'gla_b_a': nrm(ks[11], (DEPTH, GROUP_W), 0.1),
        'gla_norm': 1.0 + nrm(ks[12], (DEPTH, GROUP_W), 0.1),
        'conv_w': nrm(ks[13], (DEPTH, CONV_W, GROUP_W), CONV_W ** -0.5),
        'hgrn_gamma': nrm(ks[14], (DEPTH, GROUP_W), 1.0),
        'hgrn_norm': 1.0 + nrm(ks[15], (DEPTH, GROUP_W), 0.1),
        'pool_w': nrm(ks[16], (DEPTH, len(POOL_WINDOWS), POOL_GROUP, POOL_GROUP), POOL_GROUP ** -0.5),
        'pool_scale': 1.0 + nrm(ks[17], (DEPTH, GROUP_W), 0.1),
        'w_out': nrm(ks[18], (DEPTH, D_MIX, D_MODEL), D_MIX ** -0.5),
    }

def reference(x_prompt, x_sample, state_gla, state_conv, state_hgrn, state_pool,
              meta_tokens, norm_pre, norm_post, w_in, gla_w_a2, gla_b_a, gla_norm,
              conv_w, hgrn_gamma, hgrn_norm, pool_w, pool_scale, w_out):
    lb = _lower_bounds(hgrn_gamma)
    weights = (norm_pre, norm_post, w_in, gla_w_a2, gla_b_a, gla_norm, conv_w,
               hgrn_norm, pool_w, pool_scale, w_out)
    bp = x_prompt.shape[0]
    dt = x_prompt.dtype
    meta = jnp.broadcast_to(meta_tokens.astype(dt)[None], (bp, N_META, D_MODEL))
    hp = jnp.concatenate([meta, x_prompt], axis=1)
    hs = x_sample
    z_rec = jnp.zeros((bp, N_HEADS, HEAD_K, HEAD_V), dt)
    z_conv = jnp.zeros((bp, CONV_W - 1, GROUP_W), dt)
    z_pool = jnp.zeros((bp, POOL_BUF, GROUP_W), dt)
    pg, pc, ph, pp = [], [], [], []
    sg, sc, sh, sp = [], [], [], []
    for l in range(DEPTH):
        hp, a, b, c, d = _layer(hp, l, z_rec, z_conv, z_rec, z_pool, 0, lb, *weights)
        pg.append(a); pc.append(b); ph.append(c); pp.append(d)
        hs, a, b, c, d = _layer(hs, l, state_gla[l], state_conv[l], state_hgrn[l], state_pool[l],
                                PAST_LEN, lb, *weights)
        sg.append(a); sc.append(b); sh.append(c); sp.append(d)
    y_prompt = hp[:, N_META:]
    return (y_prompt, hs, jnp.stack(pg), jnp.stack(pc), jnp.stack(ph), jnp.stack(pp),
            jnp.stack(sg), jnp.stack(sc), jnp.stack(sh), jnp.stack(sp))


_drawn_inputs = setup_inputs


def setup_inputs(seed=0):
    import zlib

    import numpy as np

    out = dict(_drawn_inputs(seed))
    spreads = {}
    factors = {}
    for name, (base, spread) in spreads.items():
        noise = np.random.default_rng([zlib.crc32(name.encode()), seed]).standard_normal(out[name].shape)
        drawn = base * np.exp(spread * noise) if base else spread * noise
        out[name] = __import__('jax').numpy.asarray(drawn.astype(out[name].dtype))
    for name, factor in factors.items():
        out[name] = (out[name] * factor).astype(out[name].dtype)
    return out
```

```python
from contextlib import ExitStack

import concourse.bass as bass
from concourse import mybir

F32 = mybir.dt.float32
F16 = mybir.dt.float16
BF16 = mybir.dt.bfloat16
U8 = mybir.dt.uint8
ACT = mybir.ActivationFunctionType
ALU = mybir.AluOpType

D = 1024
KD = D // 128
GW = 256
HK = 64
RANK = 16
SEQ = 2048
META = 16
DB, DS = 8, 4
T0 = META + DB * DS
TT = 256
CH = 128
NT = SEQ // TT
POOLB = 15
EPS = 1e-6
SH = 16.0
SW = 256.0
CS = 1.0 / (SH * SW)
OS = 1.0 / SW
LEVELS = (64, 32, 16, 8, 4, 2, 1)
NL = len(LEVELS) + 1
SCALE = (1.0 / 16.0, 1.0)

COL = dict(a_q=0, a_k=256, a_v=512, a_lr=768, a_z=784, b_b=1040, b_c=1296, b_v=1552, b_z=1808,
           c_q=2064, c_f=2320, c_i=2576, c_z=2832, d_v=3088, d_z=3344)
DIN = 3600
ORDER = ("a_q", "a_k", "a_v", "c_i", "c_f", "c_q", "b_c", "b_v", "b_b", "b_z", "d_v", "d_z", "a_z", "c_z")
AT = {g: n * GW for n, g in enumerate(ORDER)}
FILLS = ("lr", "a_q", "la", "a_k", "vi0", "vi1", "c_f", "c_q", "b_c", "b_v", "b_b", "b_z", "d_v", "d_z",
         "a_z", "c_z")
READER = dict(lr=("lr", 1), a_q=("q", 1), la=("la", 2), a_k=("k", 1), vi0=("vi", 1), vi1=("vi", 2),
              c_f=("cf", 1), c_q=("cq", 1), b_c=("bc", 1), b_v=("ub", 1), b_b=("bb", 1), b_z=("z", 1),
              d_v=("ud", 1), d_z=("z", 2), a_z=("z", 3), c_z=("z", 4))
NF = len(FILLS)
LB0 = 2 + META + DB * (2 + DS)
LD0 = 32 + DB * (POOLB + DS)
N_CONST = 14
N_ZERO = 11

SIGNALS = dict(
    xin=32,
    ssx=2, rln=2, rs=2,
    xn=2,
    xt=4,
    hhi=4, hlo=4,
    pj=NF,
    lr=1, q=1, k=1, vi=2, bc=1, ud=1, z=4,
    la=2, cf=1, cq=1, ub=1, bb=1,
    ab=7, ex=7, lg=7, ls=7, sg=5,
    kcs=1, kc=1, qc=1,
    bsc=2,
    gs=28, ge=14, gm=28,
    sc=2 * NL * 2,
    am=2 * NL * 2,
    eq=2, qt=2, dc=2,
    ks=2, ke=2, kh=2,
    kt=2, kte=2, up=2,
    st=16,
    o=4, sq=2, ns=2, nl=2, nr=2, on=4,
    hz=4,
    cv=6, wn=4, pd=4, po=1, od=2,
    gz=4, mg=4, mhi=4, mlo=4,
    yp=2, ss=2, yln=2, yr=2,
    yg=2, xre=32, yo=2, yst=32,
)


def program(nc, a, outs):
    ctx = ExitStack()
    with ctx:
        def sb(name, shape, dt=F32):
            return ctx.enter_context(nc.sbuf_tensor(name, shape, dt))

        def sem(name):
            return ctx.enter_context(nc.semaphore(name))

        w_hi = sb("w_hi", [128, KD, len(ORDER) * GW], F16)
        w_lo = sb("w_lo", [128, KD, len(ORDER) * GW], F16)
        w_lr = sb("w_lr", [128, KD, 2 * RANK], F16)
        wo_hi = sb("wo_hi", [128, KD, D], F16)
        wo_lo = sb("wo_lo", [128, KD, D], F16)
        h_hi = sb("h_hi", [128, KD, TT], F16)
        h_lo = sb("h_lo", [128, KD, TT], F16)
        m_hi = sb("m_hi", [128, KD, TT], F16)
        m_lo = sb("m_lo", [128, KD, TT], F16)
        xbuf = sb("xbuf", [128, D])
        gpost = sb("gpost", [128, D])
        G = [sb(f"G{n}", [128, 2, TT]) for n in range(2)]
        A = [sb(f"A{n}", [128, 4, CH]) for n in range(2)]
        VI = sb("VI", [128, 2, 2 * GW])
        S = [[sb(f"S{br}{n}", [128, 2, 128]) for n in range(2)] for br in range(2)]
        Q = [sb(f"Q{br}", [128, 2, TT]) for br in range(2)]
        K = [sb(f"K{br}", [128, 2, TT]) for br in range(2)]
        B = sb("B", [128, 2, TT])
        X1, X2, X3, X4 = (sb(f"X{n}", [128, 2, TT + 16]) for n in range(1, 5))
        ident = sb("ident", [128, 128])
        bones = sb("bones", [128, 128])
        masks = sb("masks", [128, 8 * 64], U8)
        eye = sb("eye", [128, CH], U8)
        masks0 = sb("masks0", [T0, 4 * 24 + T0], U8)
        keep = sb("keep", [128, TT], U8)
        keep0 = sb("keep0", [128, T0], U8)
        rcnt = sb("rcnt", [128, 2, META + 1])
        pw = sb("pw", [128, 2, 128])
        a2 = sb("a2", [2 * RANK, GW])
        seqm = sb("seqm", [T0, DB + 1])
        vec = sb("vec", [128, 7, 2])
        gpre = sb("gpre", [128, KD])
        cst = sb("cst", [128, 1])
        sx = sb("sx", [128, 2])
        sy = sb("sy", [128, 2])
        dec = sb("dec", [128, 2, 9])
        tailB = sb("tailB", [128, 2, 2])
        tailD = sb("tailD", [128, 2, POOLB])
        TD = K[0][:, :, 64:64 + DB * POOLB].rearrange("p j (b w) -> p j b w", b=DB)
        TB = K[0][:, :, 192:192 + DB * 2].rearrange("p j (b w) -> p j b w", b=DB)
        tl = K[1][:, :, 64:112]
        mask_f = [Q[0][:, :, :].rearrange("p j t -> p (j t)"), K[0][0:T0, 0, 0:4 * 24 + T0],
                  K[1][:, 0, 0:TT], K[1][:, 1, 0:T0]]
        KTS = [Q[n][:, :, 64:192] for n in range(2)]
        X5 = X3[:, :, :].rearrange("p j t -> p (j t)")

        def ps(name):
            return ctx.enter_context(nc.psum_tensor(name, [128, 512], F32))

        pj = [ps("pj0"), ps("pj1")]
        SC = [ps("sc0"), ps("sc1")]
        M0, M1 = ps("m0"), ps("m1")
        op = ctx.enter_context(nc.psum_tensor("op", [128, D], F32))

        s = {n: sem("s_" + n) for n in SIGNALS}
        once = {n: sem("o_" + n) for n in (
            "const0", "const", "wld0", "wld1", "wmul", "whi", "wlo", "lrw", "wlr", "wold", "wohi", "wolo", "zero", "cstd",
            "tin", "tT", "wlrh", "tcp", "smp", "sdec", "vm", "su", "sv", "sout", "tl", "lT", "lcp", "fin", "pd0", "pp", "msk", "aa", "dd")}

        stage = [wo_hi[:, 4 * n:4 * n + 4, :].rearrange("p k n -> p (k n)").bitcast(F32)
                 .rearrange("p (k n) -> p k n", k=KD) for n in range(2)]
        SS = [wo_lo[:, 4 * br:4 * br + 4, :].rearrange("p k n -> p (k n)").bitcast(F32)
              .rearrange("p (b j v) -> p b j v", b=DB, j=2) for br in range(2)]
        tin = m_lo[:, :, :].rearrange("p k n -> p (k n)").bitcast(F32)
        junk = G[0][:, :, :].rearrange("p j t -> p (j t)").bitcast(BF16)

        def nth(name, i, k):
            v = i * SIGNALS[name] + k
            assert not isinstance(v, int) or v > 0, (name, i, k)
            return v

        given, last = {}, {}

        def give(eng, i, name, n):
            given[name] = given.get(name, 0) + n
            last[eng.engine] = (s[name], name, given[name])
            return s[name], n

        def give1(eng, name):
            given["o_" + name] = given.get("o_" + name, 0) + 1
            last[eng.engine] = (once[name], None, given["o_" + name])
            return once[name], 1

        def own(eng, i):
            which, name, n = last[eng.engine]
            return which, (nth(name, i, n) if name else n)

        def begin(eng, i, names, end):
            for name in names:
                assert given.get(name, SIGNALS[name]) == SIGNALS[name], name
                given[name] = 0
            if not (isinstance(i, int) and i == 0):
                last[eng.engine] = (s[end], end, 0)

        block = ctx.enter_context(nc.Block())
        dve, act, pool, pe = nc.vector, nc.scalar, nc.gpsimd, nc.tensor
        VB_A, V_GA, V_GC, V_PS, V_CW = 0, 1, 2, 3, 4

        def dims(i):
            first = isinstance(i, int) and i == 0
            return first, (T0 if first else TT), (1 if first else 2), (T0 if first else CH)


        def half(t, hh):
            return t[64 * hh:64 * hh + 64]

        def seqs(t, at, n, w, lo, hi):
            return t[:, :, at:at + n * w].rearrange("p j (b w) -> p j b w", w=w)[:, :, :, lo:hi]

        def split(t, i, lv):
            h = LEVELS[lv]
            first, T, NC, C = dims(i)
            if first:
                n = META if h >= 4 else T0
                return t[:, :, 0:n].rearrange("p j (b w) -> p j b w", w=2 * h), n
            return t[:, :, :].rearrange("p j (b w) -> p (j b) w", w=2 * h), T

        def levels(i):
            return [lv for lv in range(NL - 1) if not (isinstance(i, int) and i == 0 and LEVELS[lv] > META // 2)]

        def load_x(sp, i):
            first, T, NC, C = dims(i)
            if first:
                sp.dma_start(xbuf[0:META, :], a["meta_tokens"]).then_inc(s["xin"], 16)
                sp.dma_start(xbuf[META:T0, :], a["x_sample"].rearrange("b t d -> (b t) d")).then_inc(s["xin"], 16)
                return
            for c in range(2):
                if c == 0:
                    sp.wait_ge(s["yst"], nth("yst", i, 0))
                else:
                    sp.wait_ge(s["xt"], nth("xt", i, 2))
                sp.dma_start(xbuf[:, :], a["x_prompt"][bass.ds((i - 1) * TT + c * CH, CH), :]).then_inc(s["xin"], 16)

        def finish(sp, i):
            first, T, NC, C = dims(i)
            if first:
                sp.wait_ge(once["wolo"], KD)
                sp.dma_start(xbuf[0:META, :], a["meta_tokens"]).then_inc(s["xre"], 16)
                sp.dma_start(xbuf[META:T0, :], a["x_sample"].rearrange("b t d -> (b t) d")).then_inc(s["xre"], 16)
                sp.wait_ge(s["yo"], nth("yo", i, 2))
                for n in range(2):
                    sp.dma_start(outs["y_sample"].rearrange("b t d -> (b t) d")[16 * n:16 * n + 16, :],
                                 xbuf[META + 16 * n:META + 16 * n + 16, :]).then_inc(s["yst"], 16)
                return
            for c in range(2):
                if c == 0:
                    sp.wait_ge(s["xt"], nth("xt", i, 4))
                else:
                    sp.wait_ge(s["yst"], nth("yst", i, 16))
                src = bass.ds((i - 1) * TT + c * CH, CH)
                sp.dma_start(xbuf[:, :], a["x_prompt"][src, :]).then_inc(s["xre"], 16)
                sp.wait_ge(s["yo"], nth("yo", i, c + 1))
                sp.dma_start(outs["y_prompt"][src, :], xbuf[:, :]).then_inc(s["yst"], 16)

        @block.sync
        def _(sp):
            load_x(sp, 0)
            n_const = 0

            def const(dst, src):
                nonlocal n_const
                sp.dma_start(dst, src).then_inc(once["const"], 16)
                n_const += 1

            sp.dma_start(ident[:, :], a["c_ident"]).then_inc(once["const0"], 16)
            sp.dma_start(bones[:, :], a["c_bones"]).then_inc(once["const0"], 16)
            sp.dma_start(gpre[:, :], a["norm_pre"]).then_inc(once["const0"], 16)
            w_src = a["w_in"].rearrange("(k p) n -> p k n", p=128)
            sp.dma_start(B[:, 0, 0:KD * RANK].rearrange("p (k n) -> p k n", k=KD),
                         w_src[:, :, COL["a_lr"]:COL["a_lr"] + RANK]).then_inc(once["lrw"], 16)

            def group(n):
                if n >= 2:
                    sp.wait_ge(once["whi"], n - 1)
                    sp.wait_ge(once["wlo"], n - 1)
                g = COL[ORDER[n]]
                sp.dma_start(stage[n % 2], w_src[:, :, g:g + GW]).then_inc(once["wld%d" % (n % 2)], 16)

            group(0)
            group(1)
            for dst, name in ((mask_f[0], "c_masks"), (mask_f[1], "c_masks0"), (mask_f[2], "c_keep"), (mask_f[3], "c_keep0"),
                              (rcnt[:, :, :], "c_rcnt"), (seqm[:, :], "c_seqm"),
                              (a2[0:RANK, :], "gla_w_a2"), (a2[RANK:2 * RANK, :], "gla_w_a2")):
                const(dst, a[name])
            const(vec[:, :, :], a["vectors"])
            const(gpost[:, :], a["norm_post"].unsqueeze(0).broadcast_to([128, D]))
            sp.wait_ge(once["zero"], N_ZERO)
            for g in range(4):
                const(pw[64 * (g % 2):64 * (g % 2) + 64, g // 2, 64 * (g % 2):64 * (g % 2) + 64], a["pool_w"][g])
            assert n_const == N_CONST
            sp.dma_start(tin[0:DB * POOLB, 0:GW], a["state_pool"].rearrange("b t c -> (b t) c")).then_inc(once["tin"], 16)
            sp.dma_start(tin[0:DB * 2, GW:2 * GW], a["state_conv"].rearrange("b t c -> (b t) c")).then_inc(once["tin"], 16)
            for br, name in enumerate(("state_gla", "state_hgrn")):
                for hh in range(2):
                    for j in range(2):
                        sp.dma_start(half(SS[br], hh)[:, :, j, 64 * hh:64 * hh + 64],
                                     a[name][:, 2 * j + hh, :, :].rearrange("b k v -> k b v")
                                     ).then_inc(once["smp"], 16)
            for n in range(2, len(ORDER)):
                group(n)
            sp.dma_start(outs["pool_sample"][:, 0:POOLB - DS, :], a["state_pool"][:, DS:POOLB, :]).then_inc(once["sout"], 16)
            sp.wait_ge(once["lcp"], 2)
            sp.dma_start(outs["conv_sample"].rearrange("b t c -> (b t) c"), X5[0:DB * 2, 0:GW]).then_inc(once["sout"], 16)
            sp.dma_start(outs["pool_sample"][:, POOLB - DS:POOLB, :], X5[0:DB * DS, GW:2 * GW]).then_inc(once["sout"], 16)
            sp.wait_ge(once["sv"], 4 * DB)
            for br, name in enumerate(("gla_sample", "hgrn_sample")):
                for hh in range(2):
                    for j in range(2):
                        sp.dma_start(outs[name][:, 2 * j + hh, :, :].rearrange("b k v -> k b v"),
                                     half(SS[br], hh)[:, :, j, 64 * hh:64 * hh + 64]).then_inc(once["sout"], 16)
            sp.wait_ge(s["xt"], nth("xt", 0, 4))
            for k in range(KD):
                if k >= 1:
                    sp.wait_ge(once["wohi"], k)
                    sp.wait_ge(once["wolo"], k)
                sp.dma_start(xbuf[:, :], a["w_out"][128 * k:128 * k + 128, :]).then_inc(once["wold"], 16)
            finish(sp, 0)
            with sp.Fori(1, NT + 1) as i:
                load_x(sp, i)
                finish(sp, i)
            sp.wait_ge(s["st"], nth("st", NT, 16))
            for br, name in enumerate(("gla_prompt", "hgrn_prompt")):
                for hh in range(2):
                    for j in range(2):
                        sp.dma_start(outs[name][2 * j + hh, :, :],
                                     half(S[br][0], hh)[:, j, 64 * hh:64 * hh + 64]).then_inc(once["fin"], 16)
            sp.wait_ge(once["lcp"], 4)
            sp.dma_start(outs["conv_prompt"], X5[0:2, 0:GW]).then_inc(once["fin"], 16)
            sp.dma_start(outs["pool_prompt"], X5[0:POOLB, GW:2 * GW]).then_inc(once["fin"], 16)
            sp.wait_ge(s["yst"], 32 * (NT + 1))
            sp.wait_ge(once["sout"], 16 * 11)
            sp.wait_ge(once["fin"], 16 * 10)

        def pool_levels(i, br):
            first, T, NC, C = dims(i)
            todo = levels(i)
            for lv in range(NL - 1):
                n = 14 * br + 2 * lv
                if lv not in todo:
                    continue
                h, g = LEVELS[lv], G[lv % 2]
                Bv, _ = split(B, i, lv)
                Gv, _ = split(g, i, lv)
                Qv, _ = split(Q[br], i, lv)
                Kv, _ = split(K[br], i, lv)
                pre = (slice(None),) * (3 if first else 2)
                L, R = pre + (slice(0, h),), pre + (slice(h, 2 * h),)
                mid = Bv[pre + (slice(h - 1, h),)].broadcast_to(list(Bv[L].shape))
                if lv == todo[0]:
                    pool.wait_ge(s["bsc"], nth("bsc", i, br + 1))
                if lv in todo[:2]:
                    if not first or br:
                        pool.wait_ge(s["up"], nth("up", i, br))
                    if not first or br:
                        pool.wait_ge(s["qt"], nth("qt", i, br))
                    pool.wait_ge(s["ssx"], nth("ssx", i, 2))
                else:
                    pool.wait_ge(s["sc"], nth("sc", i, 2 * NL * br + 2 * (lv - 1)))
                late = 14 if lv == todo[0] and br == 0 else 0
                skip = (2 * todo[0]) if lv == todo[0] else 0
                pool.wait_ge(*own(pool, i))
                pool.tensor_tensor(Gv[R], Bv[R], mid, ALU.subtract).then_inc(*give(pool, i, "gs", 1 + skip))
                pool.wait_ge(*own(pool, i))
                pool.tensor_tensor(Gv[L], mid, Bv[L], ALU.subtract).then_inc(*give(pool, i, "gs", 1))
                pool.wait_ge(s["ge"], nth("ge", i, 7 * br + lv + 1))
                if lv == todo[0]:
                    if br == 0:
                        pool.wait_ge(s["q"], nth("q", i, 1))
                        pool.wait_ge(s["k"], nth("k", i, 1))
                    else:
                        pool.wait_ge(s["qc"], nth("qc", i, 1))
                        pool.wait_ge(s["kc"], nth("kc", i, 1))
                pool.wait_ge(*own(pool, i))
                pool.tensor_tensor(Gv[R], Gv[R], Qv[R], ALU.mult).then_inc(*give(pool, i, "gm", 1 + skip))
                pool.wait_ge(*own(pool, i))
                pool.tensor_tensor(Gv[L], Gv[L], Kv[L], ALU.mult).then_inc(*give(pool, i, "gm", 1))

        def pool_key(i, br):
            first, T, NC, C = dims(i)
            g = G[0]
            pool.wait_ge(s["sc"], nth("sc", i, 2 * NL * br + 14))
            if first:
                pool.wait_ge(*own(pool, i))
                pool.tensor_tensor(g[:, :, 0:META], B[:, :, META - 1:META].broadcast_to([128, 2, META]),
                                   B[:, :, 0:META], ALU.subtract).then_inc(*give1(pool, "pp"))
                new = seqs(B, META, DB, DS, 0, DS)
                pool.wait_ge(*own(pool, i))
                pool.tensor_tensor(seqs(g, META, DB, DS, 0, DS), new[:, :, :, DS - 1:DS].broadcast_to([128, 2, DB, DS]),
                                   new, ALU.subtract).then_inc(*give(pool, i, "ks", 1))
            else:
                Bc = B[:, :, :].rearrange("p j (c t) -> p (j c) t", c=2)
                pool.wait_ge(*own(pool, i))
                pool.tensor_tensor(g[:, :, :].rearrange("p j (c t) -> p (j c) t", c=2),
                                   Bc[:, :, CH - 1:CH].broadcast_to([128, 4, CH]), Bc, ALU.subtract).then_inc(*give(pool, i, "ks", 1))
            pool.wait_ge(s["ke"], nth("ke", i, br + 1))
            pool.wait_ge(s["sc"], nth("sc", i, 2 * NL * (br + 1)))
            pool.wait_ge(*own(pool, i))
            pool.tensor_tensor(K[br][:, :, 0:T], K[br][:, :, 0:T], g[:, :, 0:T], ALU.mult).then_inc(*give(pool, i, "kh", 1))

        def pool_tile(i):
            begin(pool, i, 'gs gm ks kh'.split(), 'kh')
            for br in range(2):
                pool_levels(i, br)
                pool_key(i, br)

        @block.gpsimd
        def _(_pool):
            i = 0
            for n, t in enumerate((A[0], A[1], S[0][0], S[0][1], S[1][0], S[1][1], pw, SS[0], SS[1], X3, X4)):
                pool.memset(t[:], 0.0).then_inc(*give1(pool, "zero"))
            pool.wait_ge(once["const0"], 16 * 3)
            for n in range(len(ORDER)):
                pool.wait_ge(once["wld%d" % (n % 2)], 16 * (n // 2 + 1))
                pool.wait_ge(*own(pool, i))
                pool.tensor_tensor(stage[n % 2], stage[n % 2], gpre[:, :].unsqueeze(2).broadcast_to([128, KD, GW]),
                                   ALU.mult).then_inc(*give1(pool, "wmul"))
            pool_tile(0)
            with pool.Fori(1, NT + 1) as i:
                pool_tile(i)

        def proj(i, f):
            first, T, NC, C = dims(i)
            name, bank = FILLS[f], pj[f % 2]
            who, cnt = READER[FILLS[(f - 2) % NF]]
            if not first or f >= 2:
                pe.wait_ge(s[who], nth(who, i, cnt if f >= 2 else cnt - SIGNALS[who]))
            if name == "lr":
                if first:
                    pe.wait_ge(once["wlr"], 2)
                for k in range(KD):
                    for n, h in enumerate((h_hi, h_lo)):
                        m = pe.matmul(bank[0:2 * RANK, 0:T], w_lr[:, k, :], h[:, k, 0:T],
                                      start=(k == 0 and n == 0), stop=(k == KD - 1 and n == 1))
            elif name == "la":
                pe.wait_ge(s["lr"], nth("lr", i, 1))
                if first:
                    pe.wait_ge(once["const"], 16 * N_CONST)
                for j in range(2):
                    m = pe.matmul(bank[:, j * T:(j + 1) * T], a2[:, 128 * j:128 * j + 128], X3[0:2 * RANK, 0, 0:T],
                                  start=True, stop=True)
            elif name in ("vi0", "vi1"):
                c = int(name[2])
                if first and c == 1:
                    m = pe.matmul(bank[0:32, 0:4], ident[:, 0:32], ident[:, 0:4], start=True, stop=True)
                    m.then_inc(s["pj"], 1)
                    return
                if first:
                    pe.wait_ge(once["whi"], 4)
                    pe.wait_ge(once["wlo"], 4)
                at = AT["a_v"]
                passes = ((h_hi, w_hi), (h_hi, w_lo), (h_lo, w_hi))
                for n, (h, w) in enumerate(passes):
                    for k in range(KD):
                        m = pe.matmul(bank[0:C, :], h[:, k, c * CH:c * CH + C], w[:, k, at:at + 2 * GW],
                                      start=(n == 0 and k == 0), stop=(n == 2 and k == KD - 1))
            else:
                at = AT[name]
                if first:
                    pe.wait_ge(once["whi"], at // GW + 1)
                    pe.wait_ge(once["wlo"], at // GW + 1)
                for j in range(2):
                    for n, (w, h) in enumerate(((w_hi, h_hi), (w_hi, h_lo), (w_lo, h_hi))):
                        for k in range(KD):
                            m = pe.matmul(bank[:, j * T:(j + 1) * T], w[:, k, at + 128 * j:at + 128 * j + 128],
                                          h[:, k, 0:T], start=(n == 0 and k == 0), stop=(n == 2 and k == KD - 1))
            m.then_inc(s["pj"], 1)

        def transpose_x(i):
            first, T, NC, C = dims(i)
            if first:
                pe.wait_ge(once["const0"], 16 * 3)
            for c in range(NC):
                pe.wait_ge(s["xn"], nth("xn", i, (c + 1) * (2 // NC)))
                for half_ in range(2):
                    if c == 0:
                        if not first:
                            pe.wait_ge(s["yo"], nth("yo", i, 0))
                    else:
                        pe.wait_ge(s["hlo"], nth("hlo", i, 2 * (c - 1) + half_ + 1))
                    for k in range(4):
                        m = pe.transpose(op[:, 512 * half_ + 128 * k:512 * half_ + 128 * k + C],
                                         xbuf[0:C, 128 * (4 * half_ + k):128 * (4 * half_ + k) + 128], ident[0:C, 0:C])
                    m.then_inc(s["xt"], 2 // NC)

        def scores(i, br, lv):
            first, T, NC, C = dims(i)
            unit = 2 * NL * br + 2 * lv
            for hh in range(2):
                if lv not in levels(i) and lv < NL - 1:
                    continue
                before = 2 * NL * br if lv == levels(i)[0] else unit
                if not first or before:
                    pe.wait_ge(s["am"], nth("am", i, before - 2 + hh + 1))
                if lv < NL - 1:
                    if hh == 0:
                        pe.wait_ge(s["gm"], nth("gm", i, 14 * br + 2 * lv + 2))
                    h, g = LEVELS[lv], G[lv % 2]
                    for c in range(NC):
                        for j in range(2):
                            if first:
                                n = META if h >= 4 else T0
                                L = half(g, hh)[:, j, 0:n]
                            else:
                                n = CH
                                L = half(g, hh)[:, j, c * CH:c * CH + CH]
                            R = L.rearrange("p (b w) -> p b w", w=2 * h)[:, :, h:2 * h]
                            at = (2 * c + j) * 64
                            out = SC[hh][0:n, at:at + n // 2].rearrange("p (b w) -> p b w", w=h)
                            m = pe.matmul(out, L, R, start=True, stop=True)
                else:
                    if hh == 0 and br == 0:
                        pe.wait_ge(s["q"], nth("q", i, 1))
                        pe.wait_ge(s["k"], nth("k", i, 1))
                    for c in range(NC):
                        for j in range(2):
                            at = (2 * c + j) * 128
                            m = pe.matmul(SC[hh][0:C, at:at + C], half(K[br], hh)[:, j, c * CH:c * CH + C],
                                          half(Q[br], hh)[:, j, c * CH:c * CH + C], start=True, stop=True)
                skip = 2 * levels(i)[0] if lv == levels(i)[0] and hh == 0 else 0
                m.then_inc(s["sc"], 1 + skip)

        def keys(i, br):
            first, T, NC, C = dims(i)
            pe.wait_ge(s["kh"], nth("kh", i, br + 1))
            if not first:
                pe.wait_ge(s["on"], nth("on", i, 2 * br))
            for c in range(NC):
                for j in range(2):
                    m = pe.transpose(M0[0:C, 128 * (2 * c + j):128 * (2 * c + j) + 128],
                                     K[br][:, j, c * CH:c * CH + C], ident[:, :])
            m.then_inc(s["kt"], 1)
            pe.wait_ge(s["kte"], nth("kte", i, br + 1))
            pe.wait_ge(s["vi"], nth("vi", i, 2))
            if not first or br:
                pe.wait_ge(s["nl"], nth("nl", i, br))
            KT = G[1][:, :, :].rearrange("p j t -> p (j t)")
            n = META if first else CH
            for c in range(NC):
                for j in range(2):
                    cj = 128 * (2 * c + j)
                    v = GW * br + 128 * j
                    m = pe.matmul(M1[:, cj:cj + 128], KT[0:n, cj:cj + 128], VI[0:n, c, v:v + 128], start=True, stop=True)
            m.then_inc(s["up"], 1)

        def outputs(i, br):
            first, T, NC, C = dims(i)
            pe.wait_ge(s["am"], nth("am", i, 2 * NL * (br + 1)))
            pe.wait_ge(s["qt"], nth("qt", i, br + 1))
            if first and br == 0:
                pe.wait_ge(once["smp"], 16 * 8)
            for c in range(NC):
                for j in range(2):
                    at = j * TT + c * CH
                    for hh in range(2):
                        v = GW * br + 128 * j + 64 * hh
                        pe.matmul(half(M0, hh)[:, at:at + C], VI[0:C, c, v:v + 64], A[hh][0:C, 2 * c + j, 0:C],
                                  start=True, stop=False, skip_group_check=True)
                    if first:
                        for b in range(DB):
                            t = META + DS * b
                            m = pe.matmul(M0[:, at + t:at + t + DS], SS[br][:, b, j, :], Q[br][:, j, t:t + DS],
                                          start=False, stop=True, skip_group_check=True)
                    else:
                        if j == 0:
                            pe.wait_ge(s["st"], nth("st", i, 8 * br + 4 * c))
                        m = pe.matmul(M0[:, at:at + C], S[br][c][:, j, :], Q[br][:, j, c * CH:c * CH + C],
                                      start=False, stop=True, skip_group_check=True)
                m.then_inc(s["o"], 2 // NC)

        def pool_product(i):
            first, T, NC, C = dims(i)
            pe.wait_ge(s["pd"], nth("pd", i, 4))
            pe.wait_ge(s["st"], nth("st", i, 8))
            for j in range(2):
                if first:
                    pe.matmul(M1[:, j * TT:j * TT + META], pw[:, j, :], X1[:, j, POOLB:POOLB + META],
                              start=True, stop=True)
                    new = seqs(X1, 32, DB, POOLB + DS, POOLB, POOLB + DS)[:, j]
                    m = pe.matmul(M1[:, j * TT + META:j * TT + T0].rearrange("p (b w) -> p b w", w=DS), pw[:, j, :],
                                  new, start=True, stop=True)
                else:
                    m = pe.matmul(M1[:, j * TT:j * TT + T], pw[:, j, :], X1[:, j, POOLB:POOLB + T], start=True, stop=True)
            m.then_inc(s["po"], 1)

        def head_sums(i, br):
            first, T, NC, C = dims(i)
            pe.wait_ge(s["sq"], nth("sq", i, br + 1))
            if br == 0:
                pe.wait_ge(s["od"], nth("od", i, 2))
            else:
                pe.wait_ge(s["st"], nth("st", i, 16))
            for j in range(2):
                m = pe.matmul(M1[:, j * TT:j * TT + T], bones[:, :], X4[:, j, 0:T], start=True, stop=True)
            m.then_inc(s["ns"], 1)

        def out_product(i):
            first, T, NC, C = dims(i)
            pe.wait_ge(s["mlo"], nth("mlo", i, 4))
            if first:
                pe.wait_ge(once["wohi"], KD)
                pe.wait_ge(once["wolo"], KD)
            for c in range(NC):
                if c == 0:
                    pe.wait_ge(s["hlo"], nth("hlo", i, 4))
                else:
                    pe.wait_ge(s["yo"], nth("yo", i, 1))
                for n in range(2):
                    for p, (x, w) in enumerate(((m_hi, wo_hi), (m_hi, wo_lo), (m_lo, wo_hi))):
                        for k in range(KD):
                            m = pe.matmul(op[0:C, 512 * n:512 * n + 512], x[:, k, c * CH:c * CH + C],
                                          w[:, k, 512 * n:512 * n + 512], start=(p == 0 and k == 0),
                                          stop=(p == 2 and k == KD - 1))
                m.then_inc(s["yp"], 2 // NC)

        def pe_tile(i):
            transpose_x(i)
            pe.wait_ge(s["hlo"], nth("hlo", i, 4))
            pe.wait_ge(s["hhi"], nth("hhi", i, 4))
            for f in range(8):
                proj(i, f)
            for lv in range(NL):
                scores(i, 0, lv)
                if lv < 6:
                    proj(i, 8 + lv)
            keys(i, 0)
            outputs(i, 0)
            pool_product(i)
            for lv in range(NL):
                scores(i, 1, lv)
                if lv < 2:
                    proj(i, 14 + lv)
                if lv == 3:
                    head_sums(i, 0)
            keys(i, 1)
            outputs(i, 1)
            head_sums(i, 1)

        def tails_in():
            pe.wait_ge(once["tin"], 32)
            pe.wait_ge(once["const0"], 16 * 3)
            for j in range(2):
                pe.transpose(M0[:, 128 * j:128 * j + DB * POOLB], tin[0:DB * POOLB, 128 * j:128 * j + 128],
                             ident[0:DB * POOLB, 0:DB * POOLB])
                m = pe.transpose(M0[:, GW + 128 * j:GW + 128 * j + DB * 2], tin[0:DB * 2, GW + 128 * j:GW + 128 * j + 128],
                                 ident[0:DB * 2, 0:DB * 2])
            m.then_inc(once["tT"], 1)

        def tail_out(n, t, cols, at):
            for j in range(2):
                m = pe.transpose(M0[0:cols, at + 128 * j:at + 128 * j + 128], t[:, j, 0:cols], ident[:, :])
            m.then_inc(once["lT"], 1)

        @block.tensor
        def _(_pe):
            tails_in()
            pe.wait_ge(once["tcp"], 2)
            pe_tile(0)
            pe.wait_ge(s["on"], nth("on", 0, 4))
            pe.wait_ge(once["tl"], 2)
            tail_out(0, tl, DB * 2, 0)
            tail_out(1, tl[:, :, 16:], DB * DS, GW)
            for b in range(DB):
                pe.wait_ge(once["vm"], b + 1)
                if b == 0:
                    pe.wait_ge(s["nl"], nth("nl", 0, 2))
                else:
                    pe.wait_ge(once["sv"], 4 * b)
                for br in range(2):
                    KTb = KTS[br]
                    for j in range(2):
                        m = pe.matmul(M1[:, 128 * (2 * br + j):128 * (2 * br + j) + 128], KTb[0:T0, j, :],
                                      (X1, X2)[b % 2][0:T0, :, :].rearrange("p j t -> p (j t)")[:, GW * br + 128 * j:
                                      GW * br + 128 * j + 128], start=True, stop=True)
                m.then_inc(once["su"], 1)
            out_product(0)
            with pe.Fori(1, NT + 1) as i:
                pe_tile(i)
                out_product(i)
            pe.wait_ge(s["on"], nth("on", NT, 4))
            pe.wait_ge(once["lcp"], 2)
            tail_out(2, tailB, 2, 0)
            tail_out(3, tailD, POOLB, GW)

        def evac(i, f, out, name, scale=CS):
            first, T, NC, C = dims(i)
            act.wait_ge(s["pj"], nth("pj", i, f + 1))
            act.wait_ge(*own(act, i))
            act.activation(out, pj[f % 2][:, 0:2 * T].rearrange("p (j t) -> p j t", j=2), ACT.Copy,
                           scale=scale).then_inc(*give(act, i, name, 1))

        def log_gate(i, n, E):
            first, T, NC, C = dims(i)
            act.wait_ge(s["ab"], nth("ab", i, n + 1))
            act.wait_ge(*own(act, i))
            act.activation(E[:, :, 0:T], E[:, :, 0:T], ACT.Exp, scale=-1.0).then_inc(*give(act, i, "ex", 1))
            act.wait_ge(s["ex"], nth("ex", i, n + 1))
            act.wait_ge(*own(act, i))
            act.activation(E[:, :, 0:T], E[:, :, 0:T], ACT.Ln, bias=1.0).then_inc(*give(act, i, "lg", 1))

        def sigmoid(i, n, E):
            first, T, NC, C = dims(i)
            act.wait_ge(s["ls"], nth("ls", i, n + 1))
            act.wait_ge(*own(act, i))
            act.activation(E[:, :, 0:T], E[:, :, 0:T], ACT.Exp).then_inc(*give(act, i, "sg", 1))

        def level_exp(i, br, lv):
            if lv not in levels(i):
                return
            Gv, n = split(G[lv % 2], i, lv)
            act.wait_ge(s["gs"], nth("gs", i, 14 * br + 2 * lv + 2))
            g = G[lv % 2][:, :, 0:n]
            skip = lv if lv == levels(i)[0] else 0
            act.wait_ge(*own(act, i))
            act.activation(g, g, ACT.Exp, scale=SCALE[br]).then_inc(*give(act, i, "ge", 1 + skip))

        def decays(i, br):
            first, T, NC, C = dims(i)
            act.wait_ge(s["sc"], nth("sc", i, 2 * NL * br + 12))
            act.wait_ge(*own(act, i))
            act.activation(G[1][:, :, 0:T], B[:, :, 0:T], ACT.Exp, scale=SCALE[br]).then_inc(*give(act, i, "eq", 1))
            ends = B[:, :, META - 1:T0:DS] if first else B[:, :, CH - 1:TT:CH]
            if not first:
                act.wait_ge(s["st"], nth("st", i, 8 * br))
            act.wait_ge(*own(act, i))
            act.activation(dec[:, :, 0:9 if first else 2], ends, ACT.Exp, scale=SCALE[br]).then_inc(*give(act, i, "dc", 1))
            act.wait_ge(s["ks"], nth("ks", i, br + 1))
            act.wait_ge(*own(act, i))
            act.activation(G[0][:, :, 0:T], G[0][:, :, 0:T], ACT.Exp, scale=SCALE[br]).then_inc(*give(act, i, "ke", 1))
            act.wait_ge(s["kt"], nth("kt", i, br + 1))
            act.wait_ge(s["qt"], nth("qt", i, br + 1))
            if first:
                act.wait_ge(*own(act, i))
                act.activation(KTS[br][0:T0, :, :], M0[0:T0, 0:256].rearrange("p (j n) -> p j n", j=2),
                               ACT.Copy).then_inc(*give1(act, "aa"))
                act.wait_ge(*own(act, i))
                act.activation(G[1][0:META, :, :].rearrange("p j t -> p (j t)")[:, 0:256], M0[0:META, 0:256],
                               ACT.Copy).then_inc(*give(act, i, "kte", 1))
            else:
                act.wait_ge(*own(act, i))
                act.activation(G[1][:, :, :].rearrange("p j t -> p (j t)"), M0[:, :], ACT.Copy).then_inc(*give(act, i, "kte", 1))

        def square(i, br):
            first, T, NC, C = dims(i)
            act.wait_ge(s["o"], nth("o", i, 2 * br + 2))
            act.wait_ge(s["mlo"], nth("mlo", i, 2 if br == 0 else 3))
            act.wait_ge(*own(act, i))
            act.activation(X4[:, :, 0:T], M0[:, :].rearrange("p (j t) -> p j t", j=2)[:, :, 0:T],
                           ACT.Square).then_inc(*give(act, i, "sq", 1))

        def inv_rms(i, br):
            first, T, NC, C = dims(i)
            act.wait_ge(s["ns"], nth("ns", i, br + 1))
            act.wait_ge(*own(act, i))
            act.activation(X4[:, :, 0:T], M1[:, :].rearrange("p (j t) -> p j t", j=2)[:, :, 0:T], ACT.Ln,
                           scale=1.0 / HK, bias=cst[:, 0:1]).then_inc(*give(act, i, "nl", 1))
            act.wait_ge(s["nl"], nth("nl", i, br + 1))
            act.wait_ge(*own(act, i))
            act.activation(X4[:, :, 0:T], X4[:, :, 0:T], ACT.Exp, scale=-0.5).then_inc(*give(act, i, "nr", 1))

        def mix_hi(i, n):
            first, T, NC, C = dims(i)
            at = (2, 6, 0, 4)[n]
            act.wait_ge(s["mg"], nth("mg", i, n + 1))
            if n == 0:
                if not first:
                    act.wait_ge(s["yp"], nth("yp", i, 0))
            act.wait_ge(*own(act, i))
            act.activation(m_hi[:, at:at + 2, 0:T], X4[:, :, 0:T], ACT.Copy).then_inc(*give(act, i, "mhi", 1))

        def act_tile(i):
            begin(act, i, 'ssx rln rs hhi lr q k vi bc ud z ex lg sg kc ge eq dc ke kte sq nl nr mhi ss yln yr'.split(), 'yr')
            first, T, NC, C = dims(i)
            for c in range(NC):
                k = 2 // NC
                act.wait_ge(s["xin"], nth("xin", i, 16 * (c + 1) * k))
                if c == 0:
                    if not first:
                        act.wait_ge(s["kh"], nth("kh", i, 0))
                    if not first:
                        act.wait_ge(s["xn"], nth("xn", i, 0))
                act.wait_ge(*own(act, i))
                act.activation(junk[0:C, :], xbuf[0:C, :], ACT.Square, accum_out=sx[0:C, c:c + 1]).then_inc(*give(act, i, "ssx", k))
                act.wait_ge(s["ssx"], nth("ssx", i, k * (c + 1)))
                act.wait_ge(*own(act, i))
                act.activation(sx[0:C, c:c + 1], sx[0:C, c:c + 1], ACT.Ln, scale=1.0 / D,
                               bias=cst[0:C, 0:1]).then_inc(*give(act, i, "rln", k))
                act.wait_ge(s["rln"], nth("rln", i, k * (c + 1)))
                act.wait_ge(*own(act, i))
                act.activation(sx[0:C, c:c + 1], sx[0:C, c:c + 1], ACT.Exp, scale=-0.5).then_inc(*give(act, i, "rs", k))
                for n in range(2):
                    act.wait_ge(s["xt"], nth("xt", i, k * (2 * c + n + 1) if not first else 2 * n + 2))
                    if c == 0 and n == 0:
                        if not first:
                            act.wait_ge(s["pj"], nth("pj", i, 0))
                    act.wait_ge(*own(act, i))
                    act.activation(h_hi[:, 4 * n:4 * n + 4, c * CH:c * CH + C],
                                   op[:, 512 * n:512 * n + 512].rearrange("p (k t) -> p k t", k=4)[:, :, 0:C],
                                   ACT.Copy).then_inc(*give(act, i, "hhi", k))
            act.wait_ge(s["pj"], nth("pj", i, 1))
            if not first:
                act.wait_ge(s["gz"], nth("gz", i, 0))
            act.wait_ge(*own(act, i))
            act.activation(X3[0:2 * RANK, 0, 0:T], pj[0][0:2 * RANK, 0:T], ACT.Copy, scale=CS).then_inc(*give(act, i, "lr", 1))
            if not first:
                act.wait_ge(s["sc"], nth("sc", i, 0))
            if not first:
                act.wait_ge(s["o"], nth("o", i, 0))
            if first:
                act.wait_ge(once["msk"], 5)
            evac(i, 1, Q[0][:, :, 0:T], "q", CS * HK ** -0.5)
            evac(i, 3, K[0][:, :, 0:T], "k")
            log_gate(i, 0, X2)
            for c in range(2):
                act.wait_ge(s["pj"], nth("pj", i, 5 + c))
                if c >= NC:
                    act.wait_ge(*own(act, i))
                    act.activation(VI[0:1, 1, 0:1], cst[0:1, 0:1], ACT.Copy).then_inc(*give(act, i, "vi", 1))
                    continue
                act.wait_ge(*own(act, i))
                act.activation(VI[0:C, c, :], pj[c % 2][0:C, :], ACT.Copy, scale=CS).then_inc(*give(act, i, "vi", 1))
            log_gate(i, 1, X2)
            act.wait_ge(s["kcs"], nth("kcs", i, 1))
            act.wait_ge(*own(act, i))
            act.activation(K[1][:, :, 0:T], X1[:, :, 0:T], ACT.Exp).then_inc(*give(act, i, "kc", 1))
            log_gate(i, 2, X3)
            sigmoid(i, 2, X3)
            for lv in range(NL):
                if lv < NL - 1:
                    level_exp(i, 0, lv)
                if lv == 0:
                    act.wait_ge(s["qc"], nth("qc", i, 1))
                    evac(i, 8, X3[:, :, 0:T], "bc")
                if lv == 3:
                    evac(i, 11, X1[:, :, 0:T], "z")
                if lv == 4:
                    log_gate(i, 3, X3)
                if lv == 5:
                    sigmoid(i, 3, X3)
                    mix_hi(i, 0)
                if lv == 6:
                    act.wait_ge(s["gz"], nth("gz", i, 1))
                    act.wait_ge(s["pj"], nth("pj", i, 13))
                    if first:
                        act.wait_ge(*own(act, i))
                        act.activation(X3[:, :, POOLB:POOLB + META],
                                       pj[0][:, 0:2 * T].rearrange("p (j t) -> p j t", j=2)[:, :, 0:META], ACT.Copy,
                                       scale=CS).then_inc(*give1(act, "aa"))
                        for j in range(2):
                            act.wait_ge(*own(act, i))
                            m = act.activation(seqs(X3, 32, DB, POOLB + DS, POOLB, POOLB + DS)[:, j],
                                           pj[0][:, j * T + META:j * T + T0].rearrange("p (b w) -> p b w", w=DS), ACT.Copy,
                                           scale=CS)
                        m.then_inc(*give(act, i, "ud", 1))
                    else:
                        evac(i, 12, X3[:, :, POOLB:POOLB + T], "ud")
            decays(i, 0)
            for lv in range(NL):
                if lv < NL - 1:
                    level_exp(i, 1, lv)
                if lv == 0:
                    act.wait_ge(s["po"], nth("po", i, 1))
                    evac(i, 13, X1[:, :, 0:T], "z")
                if lv == 1:
                    log_gate(i, 4, X3)
                if lv == 2:
                    sigmoid(i, 4, X3)
                if lv == 3:
                    mix_hi(i, 1)
                    square(i, 0)
                if lv == 4:
                    inv_rms(i, 0)
                    act.wait_ge(s["mg"], nth("mg", i, 2))
                    evac(i, 14, X1[:, :, 0:T], "z")
                if lv == 5:
                    log_gate(i, 5, X3)
                if lv == 6:
                    sigmoid(i, 5, X3)
                if lv == 7:
                    mix_hi(i, 2)
            decays(i, 1)
            act.wait_ge(s["mg"], nth("mg", i, 3))
            evac(i, 15, X1[:, :, 0:T], "z")
            log_gate(i, 6, X3)
            square(i, 1)
            inv_rms(i, 1)
            sigmoid(i, 6, X3)
            mix_hi(i, 3)

        def act_out(i):
            first, T, NC, C = dims(i)
            k = 2 // NC
            for c in range(NC):
                act.wait_ge(s["yp"], nth("yp", i, k * (c + 1)))
                act.wait_ge(*own(act, i))
                act.activation(junk[0:C, :], op[0:C, :], ACT.Square, scale=OS,
                               accum_out=sy[0:C, c:c + 1]).then_inc(*give(act, i, "ss", k))
                act.wait_ge(s["ss"], nth("ss", i, k * (c + 1)))
                act.wait_ge(*own(act, i))
                act.activation(sy[0:C, c:c + 1], sy[0:C, c:c + 1], ACT.Ln, scale=1.0 / D,
                               bias=cst[0:C, 0:1]).then_inc(*give(act, i, "yln", k))
                act.wait_ge(s["yln"], nth("yln", i, k * (c + 1)))
                act.wait_ge(*own(act, i))
                act.activation(sy[0:C, c:c + 1], sy[0:C, c:c + 1], ACT.Exp, scale=-0.5).then_inc(*give(act, i, "yr", k))

        @block.scalar
        def _(_act):
            i = 0
            act.preload_act_table_set("natural_log_exp_and_others")
            act.wait_ge(once["cstd"], 1)
            act.wait_ge(once["lrw"], 16)
            act.wait_ge(once["wlr"], 1)
            act.activation(w_lr[:, :, 0:RANK], B[:, 0, 0:KD * RANK].rearrange("p (k n) -> p k n", k=KD), ACT.Copy,
                           scale=SW).then_inc(*give1(act, "wlrh"))
            for n in range(len(ORDER)):
                act.wait_ge(once["wmul"], n + 1)
                act.wait_ge(*own(act, i))
                act.activation(w_hi[:, :, GW * n:GW * n + GW], stage[n % 2], ACT.Copy, scale=SW).then_inc(*give1(act, "whi"))
            act.wait_ge(once["tT"], 1)
            act.wait_ge(once["zero"], N_ZERO)
            act.wait_ge(once["msk"], 5)
            for j in range(2):
                act.wait_ge(*own(act, i))
                act.activation(TD[:, j, :, :], M0[:, 128 * j:128 * j + DB * POOLB].rearrange("p (b w) -> p b w", b=DB),
                               ACT.Copy).then_inc(*give1(act, "aa"))
                act.wait_ge(*own(act, i))
                act.activation(TB[:, j, :, :], M0[:, GW + 128 * j:GW + 128 * j + DB * 2].rearrange("p (b w) -> p b w", b=DB),
                               ACT.Copy).then_inc(*give1(act, "tcp"))
            act_tile(0)
            act.wait_ge(s["gz"], nth("gz", 0, 4))
            for n, rows in ((0, DB * 2), (1, DB * DS)):
                act.wait_ge(once["lT"], 2)
                act.wait_ge(*own(act, i))
                act.activation(X5[0:rows, GW * n:GW * n + GW], M0[0:rows, GW * n:GW * n + GW],
                               ACT.Copy).then_inc(*give1(act, "lcp"))
            for k in range(KD):
                act.wait_ge(once["wold"], 16 * (k + 1))
                if k == 0:
                    act.wait_ge(once["whi"], len(ORDER))
                    act.wait_ge(once["wlo"], len(ORDER))
                act.wait_ge(*own(act, i))
                act.activation(wo_hi[:, k, :], xbuf[:, :], ACT.Copy, scale=SW).then_inc(*give1(act, "wohi"))
            act_out(0)
            act.wait_ge(once["sout"], 16 * 11)
            with act.Fori(1, NT + 1) as i:
                act_tile(i)
                act_out(i)
            for n, rows in ((0, 2), (1, POOLB)):
                act.wait_ge(once["lT"], 4)
                act.wait_ge(*own(act, i))
                act.activation(X5[0:rows, GW * n:GW * n + GW], M0[0:rows, GW * n:GW * n + GW],
                               ACT.Copy).then_inc(*give1(act, "lcp"))

        def absolute(i, n, z, E):
            first, T, NC, C = dims(i)
            dve.wait_ge(*own(dve, i))
            dve.scalar_tensor_tensor(E[:, :, 0:T], z[:, :, 0:T], -1.0, z[:, :, 0:T], ALU.mult, ALU.max).then_inc(*give(dve, i, "ab", 1))

        def log_sigmoid(i, n, z, E):
            first, T, NC, C = dims(i)
            dve.wait_ge(s["lg"], nth("lg", i, n + 1))
            dve.wait_ge(*own(dve, i))
            dve.scalar_tensor_tensor(E[:, :, 0:T], z[:, :, 0:T], 0.0, E[:, :, 0:T], ALU.min,
                                     ALU.subtract).then_inc(*give(dve, i, "ls", 1))

        def running_sum(i, br):
            first, T, NC, C = dims(i)
            dve.wait_ge(s["ls"], nth("ls", i, br + 1))
            if br == 0:
                if not first:
                    dve.wait_ge(s["kh"], nth("kh", i, 0))
                if not first:
                    dve.wait_ge(s["eq"], nth("eq", i, 0))
                if not first:
                    dve.wait_ge(s["dc"], nth("dc", i, 0))
            else:
                dve.wait_ge(s["ks"], nth("ks", i, 1))
                dve.wait_ge(s["eq"], nth("eq", i, 1))
                dve.wait_ge(s["dc"], nth("dc", i, 1))
            for j in range(2):
                dve.wait_ge(*own(dve, i))
                m = dve.tensor_tensor_scan(B[:, j, 0:T], (keep0 if first else keep)[:, :], X2[:, j, 0:T],
                                           0.0, ALU.mult, ALU.add)
            m.then_inc(*give(dve, i, "bsc", 1))

        def copy_scores(i, br, lv):
            first, T, NC, C = dims(i)
            if lv < NL - 1 and lv not in levels(i):
                return
            for hh in range(2):
                if first:
                    dve.wait_ge(s["sc"], nth("sc", i, 2 * NL * br + 2 * lv + hh + 1))
                else:
                    dve.reg_add(sc_count, sc_count, 1)
                    dve.wait_ge(once["cstd"], 2)
                    dve.wait_ge(s["sc"], sc_count)
                if lv == levels(i)[0] and hh == 0:
                    if not first:
                        dve.wait_ge(s["o"], nth("o", i, 2 * br))
                skip = 2 * lv if lv == levels(i)[0] and hh == 0 else 0
                if lv < NL - 1:
                    h = LEVELS[lv]
                    n = (META if h >= 4 else T0) if first else CH
                    q = 2 * NC
                    mk = masks0[0:n, 24 * (lv - 3):24 * (lv - 3) + n // 2] if first else masks[:, 64 * lv:64 * lv + 64]
                    mk = mk.rearrange("p (b w) -> p b w", w=h)
                    for cj in range(q):
                        out = A[hh][0:n, cj, 0:n].rearrange("p (b w) -> p b w", w=2 * h)[:, :, h:2 * h]
                        m = dve.copy_predicated(out, mk, SC[hh][0:n, 64 * cj:64 * cj + n // 2].rearrange(
                            "p (b w) -> p b w", w=h))
                else:
                    mk = masks0[0:T0, 96:96 + T0] if first else eye[:, :]
                    q = 2 * NC
                    m = dve.copy_predicated(A[hh][0:C, 0:q, 0:C], mk.unsqueeze(1).broadcast_to([C, q, C]),
                                            SC[hh][0:C, 0:128 * q].rearrange("p (q t) -> p q t", t=128)[:, :, 0:C])
                m.then_inc(*give(dve, i, "am", 1 + skip))

        def query(i, br):
            first, T, NC, C = dims(i)
            dve.wait_ge(s["eq"], nth("eq", i, br + 1))
            dve.wait_ge(s["gm"], nth("gm", i, 14 * br + 14))
            dve.wait_ge(*own(dve, i))
            dve.tensor_tensor(Q[br][:, :, 0:T], Q[br][:, :, 0:T], G[1][:, :, 0:T], ALU.mult).then_inc(*give(dve, i, "qt", 1))

        def states(i, br):
            first, T, NC, C = dims(i)
            dve.wait_ge(s["up"], nth("up", i, br + 1))
            dve.wait_ge(s["dc"], nth("dc", i, br + 1))
            if first:
                for hh in range(2):
                    dve.wait_ge(*own(dve, i))
                    dve.tensor_copy(half(S[br][0], hh)[:, :, 64 * hh:64 * hh + 64],
                                    half(M1, hh)[:, 0:256].rearrange("p (j v) -> p j v", j=2)[:, :, 64 * hh:64 * hh + 64]
                                    ).then_inc(*give(dve, i, "st", 4))
                dve.wait_ge(s["o"], nth("o", i, 2 * br + 2))
                for hh in range(2):
                    for j in range(2):
                        Sv = half(SS[br], hh)[:, :, j, 64 * hh:64 * hh + 64]
                        dve.wait_ge(*own(dve, i))
                        dve.tensor_tensor(Sv, Sv, half(dec, hh)[:, j, 1:9].unsqueeze(2).broadcast_to([64, DB, 64]),
                                          ALU.mult).then_inc(*give1(dve, "sdec"))
                return
            for c in range(2):
                dve.wait_ge(s["o"], nth("o", i, 2 * br + c))
                if c == 1:
                    dve.wait_ge(s["st"], nth("st", i, 8 * br + 4))
                for hh in range(2):
                    for j in range(2):
                        v = slice(64 * hh, 64 * hh + 64)
                        dve.wait_ge(*own(dve, i))
                        dve.scalar_tensor_tensor(half(S[br][1 - c], hh)[:, j, v], half(S[br][c], hh)[:, j, v],
                                                 half(dec, hh)[:, j, c:c + 1],
                                                 half(M1, hh)[:, 128 * (2 * c + j) + 64 * hh:128 * (2 * c + j) + 64 * hh + 64],
                                                 ALU.mult, ALU.add).then_inc(*give(dve, i, "st", 1))

        def gate(i, n, sg):
            first, T, NC, C = dims(i)
            dve.wait_ge(s["sg"], nth("sg", i, sg))
            dve.wait_ge(*own(dve, i))
            dve.tensor_tensor(X1[:, :, 0:T], X1[:, :, 0:T], X3[:, :, 0:T], ALU.mult).then_inc(*give(dve, i, "gz", 1))
            dve.wait_ge(s["gz"], nth("gz", i, n + 1))
            dve.wait_ge(*own(dve, i))
            dve.tensor_tensor(X4[:, :, 0:T], X4[:, :, 0:T], X1[:, :, 0:T], ALU.mult).then_inc(*give(dve, i, "mg", 1))

        def mix_lo(i, n):
            first, T, NC, C = dims(i)
            at = (2, 6, 0, 4)[n]
            dve.wait_ge(s["mhi"], nth("mhi", i, n + 1))
            dve.wait_ge(*own(dve, i))
            dve.tensor_tensor(m_lo[:, at:at + 2, 0:T], X4[:, :, 0:T], m_hi[:, at:at + 2, 0:T],
                              ALU.subtract).then_inc(*give(dve, i, "mlo", 1))

        def normalise(i, br):
            first, T, NC, C = dims(i)
            dve.wait_ge(s["nr"], nth("nr", i, br + 1))
            for j in range(2):
                dve.wait_ge(*own(dve, i))
                dve.scalar_tensor_tensor(X4[:, j, 0:T], M0[:, j * TT:j * TT + T], vec[:, V_GA + br, j:j + 1],
                                         X4[:, j, 0:T], ALU.mult, ALU.mult).then_inc(*give(dve, i, "on", 1))

        def convolution(i):
            first, T, NC, C = dims(i)
            dve.wait_ge(s["pj"], nth("pj", i, 10))
            dve.wait_ge(s["bc"], nth("bc", i, 1))
            if not first:
                dve.wait_ge(s["mlo"], nth("mlo", i, 0))
            L = LB0 if first else T + 2
            if first:
                dve.wait_ge(once["tcp"], 2)
                dve.wait_ge(*own(dve, i))
                dve.tensor_copy(seqs(X4, 18, DB, 2 + DS, 0, 2), TB[:, :, :, :]).then_inc(*give(dve, i, "hz", 1))
                P = pj[1][:, 0:2 * T].rearrange("p (j t) -> p j t", j=2)
                dve.wait_ge(*own(dve, i))
                dve.scalar_tensor_tensor(X4[:, :, 2:2 + META], P[:, :, 0:META], CS, X3[:, :, 0:META], ALU.mult,
                                         ALU.mult).then_inc(*give1(dve, "dd"))
                for j in range(2):
                    dve.wait_ge(*own(dve, i))
                    m = dve.scalar_tensor_tensor(seqs(X4, 18, DB, 2 + DS, 2, 2 + DS)[:, j],
                                             P[:, j, META:T0].rearrange("p (b w) -> p b w", w=DS), CS,
                                             X3[:, j, META:T0].rearrange("p (b w) -> p b w", w=DS), ALU.mult,
                                             ALU.mult)
                m.then_inc(*give(dve, i, "ub", 1))
            else:
                dve.wait_ge(*own(dve, i))
                dve.tensor_copy(X4[:, :, 0:2], tailB[:, :, :]).then_inc(*give(dve, i, "hz", 1))
                dve.wait_ge(*own(dve, i))
                dve.scalar_tensor_tensor(X4[:, :, 2:2 + T], pj[1][:, 0:2 * T].rearrange("p (j t) -> p j t", j=2), CS,
                                         X3[:, :, 0:T], ALU.mult, ALU.mult).then_inc(*give(dve, i, "ub", 1))
            dve.wait_ge(s["ub"], nth("ub", i, 1))
            dve.wait_ge(s["hz"], nth("hz", i, 1))
            for n in range(3):
                for j in range(2):
                    w = vec[:, V_CW + n, j:j + 1]
                    if n == 0:
                        dve.wait_ge(*own(dve, i))
                        dve.tensor_scalar(X3[:, j, 0:L - 2], X4[:, j, 0:L - 2], w, None, ALU.mult).then_inc(*give(dve, i, "cv", 1))
                    else:
                        dve.wait_ge(s["cv"], nth("cv", i, 2 * (n - 1) + j + 1))
                        dve.wait_ge(*own(dve, i))
                        dve.scalar_tensor_tensor(X3[:, j, 0:L - 2], X4[:, j, n:L - 2 + n], w, X3[:, j, 0:L - 2], ALU.mult,
                                                 ALU.add).then_inc(*give(dve, i, "cv", 1))
            dve.wait_ge(*own(dve, i))
            dve.tensor_copy(tailB[:, :, :], X4[:, :, META:META + 2] if first else X4[:, :, T:T + 2]).then_inc(*give(dve, i, "hz", 1))
            if first:
                dve.wait_ge(*own(dve, i))
                dve.tensor_copy(tl[:, :, 0:16].rearrange("p j (b w) -> p j b w", w=2), seqs(X4, 18, DB, 2 + DS, 4, 6)
                                ).then_inc(*give1(dve, "tl"))

        def conv_out(i):
            first, T, NC, C = dims(i)
            dve.wait_ge(s["pj"], nth("pj", i, 11))
            dve.wait_ge(s["cv"], nth("cv", i, 6))
            dve.wait_ge(s["hz"], nth("hz", i, 2))
            P = pj[0][:, 0:2 * T].rearrange("p (j t) -> p j t", j=2)
            if first:
                dve.wait_ge(once["tl"], 1)
                dve.wait_ge(*own(dve, i))
                dve.scalar_tensor_tensor(X4[:, :, 0:META], P[:, :, 0:META], CS, X3[:, :, 0:META], ALU.mult,
                                         ALU.mult).then_inc(*give1(dve, "dd"))
                for j in range(2):
                    dve.wait_ge(*own(dve, i))
                    m = dve.scalar_tensor_tensor(X4[:, j, META:T0].rearrange("p (b w) -> p b w", w=DS),
                                             P[:, j, META:T0].rearrange("p (b w) -> p b w", w=DS), CS,
                                             seqs(X3, 18, DB, 2 + DS, 0, DS)[:, j], ALU.mult, ALU.mult)
                m.then_inc(*give(dve, i, "bb", 1))
            else:
                dve.wait_ge(*own(dve, i))
                dve.scalar_tensor_tensor(X4[:, :, 0:T], P, CS, X3[:, :, 0:T], ALU.mult, ALU.mult).then_inc(*give(dve, i, "bb", 1))

        def pooling_in(i):
            first, T, NC, C = dims(i)
            dve.wait_ge(s["gz"], nth("gz", i, 1))
            if first:
                dve.wait_ge(*own(dve, i))
                dve.memset(X3[:, :, 0:POOLB], 0.0).then_inc(*give1(dve, "dd"))
                dve.memset(X3[:, :, POOLB + META:32], 0.0).then_inc(*give1(dve, "dd"))
                dve.wait_ge(*own(dve, i))
                dve.tensor_copy(seqs(X3, 32, DB, POOLB + DS, 0, POOLB), TD[:, :, :, :]).then_inc(*give(dve, i, "hz", 1))
            else:
                dve.wait_ge(*own(dve, i))
                dve.tensor_copy(X3[:, :, 0:POOLB], tailD[:, :, :]).then_inc(*give(dve, i, "hz", 1))

        def pooling(i):
            first, T, NC, C = dims(i)
            L = LD0 if first else T + POOLB
            dve.wait_ge(s["ud"], nth("ud", i, 1))
            dve.wait_ge(s["hz"], nth("hz", i, 3))
            dve.wait_ge(s["mlo"], nth("mlo", i, 1))
            dve.wait_ge(*own(dve, i))
            dve.tensor_tensor(X1[:, :, 1:L], X3[:, :, 1:L], X3[:, :, 0:L - 1], ALU.add).then_inc(*give(dve, i, "wn", 1))
            dve.wait_ge(s["wn"], nth("wn", i, 1))
            dve.wait_ge(*own(dve, i))
            dve.tensor_tensor(X4[:, :, 3:L], X1[:, :, 3:L], X1[:, :, 1:L - 2], ALU.add).then_inc(*give(dve, i, "wn", 1))
            dve.wait_ge(s["wn"], nth("wn", i, 2))
            dve.wait_ge(*own(dve, i))
            dve.tensor_tensor(X1[:, 1, 7:L], X4[:, 1, 7:L], X4[:, 1, 3:L - 4], ALU.add).then_inc(*give(dve, i, "wn", 1))
            dve.wait_ge(s["wn"], nth("wn", i, 3))
            dve.wait_ge(*own(dve, i))
            dve.tensor_tensor(X4[:, 1, 15:L], X1[:, 1, 15:L], X1[:, 1, 7:L - 8], ALU.add).then_inc(*give(dve, i, "wn", 1))
            dve.wait_ge(s["wn"], nth("wn", i, 4))
            for n, (hh, j, src, w) in enumerate(((0, 0, X1, 2), (1, 0, X4, 4), (0, 1, X1, 8), (1, 1, X4, 16))):
                out, win, u = half(X1, hh)[:, j, 15:L], half(src, hh)[:, j, 15:L], half(X3, hh)[:, j, 15:L]
                if first:
                    m = META + 1
                    dve.wait_ge(*own(dve, i))
                    dve.tensor_tensor(out[:, 0:m], win[:, 0:m], half(rcnt, hh)[:, j, :], ALU.mult).then_inc(*give1(dve, "pd0"))
                    dve.wait_ge(once["pd0"], n + 1)
                    dve.wait_ge(*own(dve, i))
                    dve.tensor_tensor(out[:, 0:m], out[:, 0:m], u[:, 0:m], ALU.subtract).then_inc(*give1(dve, "dd"))
                    dve.wait_ge(*own(dve, i))
                    dve.scalar_tensor_tensor(out[:, m:], win[:, m:], 1.0 / w, u[:, m:], ALU.mult,
                                             ALU.subtract).then_inc(*give(dve, i, "pd", 1))
                else:
                    dve.wait_ge(*own(dve, i))
                    dve.scalar_tensor_tensor(out, win, 1.0 / w, u, ALU.mult, ALU.subtract).then_inc(*give(dve, i, "pd", 1))
            dve.wait_ge(*own(dve, i))
            dve.tensor_copy(tailD[:, :, :], X3[:, :, META:META + POOLB] if first else X3[:, :, T:T + POOLB]
                            ).then_inc(*give(dve, i, "hz", 1))
            if first:
                for j in range(2):
                    dve.wait_ge(*own(dve, i))
                    m = dve.tensor_copy(tl[:, j, 16:48].rearrange("p (b w) -> p b w", w=DS),
                                    seqs(X3, 32, DB, POOLB + DS, POOLB, POOLB + DS)[:, j])
                m.then_inc(*give1(dve, "tl"))

        def dve_tile(i):
            begin(dve, i, 'xn hlo la cf cq ub bb ab ls kcs qc bsc am qt st on hz cv wn pd od gz mg mlo yg yo'.split(), 'yo')
            first, T, NC, C = dims(i)
            k = 2 // NC
            for c in range(NC):
                dve.wait_ge(s["rs"], nth("rs", i, k * (c + 1)))
                dve.wait_ge(*own(dve, i))
                dve.tensor_scalar(xbuf[0:C, :], xbuf[0:C, :], sx[0:C, c:c + 1], SH, ALU.mult, ALU.mult).then_inc(*give(dve, i, "xn", k))
                for n in range(2):
                    dve.wait_ge(s["hhi"], nth("hhi", i, k * (2 * c + n + 1)))
                    dve.wait_ge(*own(dve, i))
                    dve.tensor_tensor(h_lo[:, 4 * n:4 * n + 4, c * CH:c * CH + C],
                                      op[:, 512 * n:512 * n + 512].rearrange("p (k t) -> p k t", k=4)[:, :, 0:C],
                                      h_hi[:, 4 * n:4 * n + 4, c * CH:c * CH + C], ALU.subtract).then_inc(*give(dve, i, "hlo", k))
            dve.wait_ge(s["pj"], nth("pj", i, 3))
            for j in range(2):
                dve.wait_ge(*own(dve, i))
                dve.tensor_scalar(X1[:, j, 0:T], pj[0][:, j * T:(j + 1) * T], vec[:, VB_A, j:j + 1], None,
                                  ALU.add).then_inc(*give(dve, i, "la", 1))
            dve.wait_ge(s["la"], nth("la", i, 2))
            if not first:
                dve.wait_ge(s["bsc"], nth("bsc", i, 0))
            absolute(i, 0, X1, X2)
            log_sigmoid(i, 0, X1, X2)
            running_sum(i, 0)
            dve.wait_ge(s["pj"], nth("pj", i, 7))
            dve.wait_ge(*own(dve, i))
            dve.tensor_scalar(X1[:, :, 0:T], pj[0][:, 0:2 * T].rearrange("p (j t) -> p j t", j=2), CS, None,
                              ALU.mult).then_inc(*give(dve, i, "cf", 1))
            dve.wait_ge(s["cf"], nth("cf", i, 1))
            dve.wait_ge(s["bsc"], nth("bsc", i, 1))
            absolute(i, 1, X1, X2)
            dve.wait_ge(s["pj"], nth("pj", i, 8))
            dve.wait_ge(*own(dve, i))
            dve.tensor_scalar(Q[1][:, :, 0:T], pj[1][:, 0:2 * T].rearrange("p (j t) -> p j t", j=2), CS, None,
                              ALU.mult).then_inc(*give(dve, i, "cq", 1))
            dve.wait_ge(s["cq"], nth("cq", i, 1))
            dve.wait_ge(s["lr"], nth("lr", i, 1))
            absolute(i, 2, Q[1], X3)
            log_sigmoid(i, 1, X1, X2)
            dve.wait_ge(s["ls"], nth("ls", i, 2))
            dve.wait_ge(*own(dve, i))
            dve.tensor_tensor(X1[:, :, 0:T], X2[:, :, 0:T], X1[:, :, 0:T], ALU.subtract).then_inc(*give(dve, i, "kcs", 1))
            log_sigmoid(i, 2, Q[1], X3)
            dve.wait_ge(s["sg"], nth("sg", i, 1))
            dve.wait_ge(*own(dve, i))
            dve.scalar_tensor_tensor(Q[1][:, :, 0:T], Q[1][:, :, 0:T], HK ** -0.5, X3[:, :, 0:T], ALU.mult,
                                     ALU.mult).then_inc(*give(dve, i, "qc", 1))
            for lv in range(NL):
                copy_scores(i, 0, lv)
                if lv == 1:
                    convolution(i)
                if lv == 2:
                    conv_out(i)
                if lv == 3:
                    dve.wait_ge(s["z"], nth("z", i, 1))
                    absolute(i, 3, X1, X3)
                if lv == 4:
                    log_sigmoid(i, 3, X1, X3)
                if lv == 5:
                    gate(i, 0, 2)
                if lv == 6:
                    mix_lo(i, 0)
                    pooling_in(i)
                if lv == 7:
                    pooling(i)
            query(i, 0)
            running_sum(i, 1)
            states(i, 0)
            for lv in range(NL):
                copy_scores(i, 1, lv)
                if lv == 0:
                    dve.wait_ge(s["po"], nth("po", i, 1))
                    for j in range(2):
                        dve.wait_ge(*own(dve, i))
                        dve.tensor_scalar(X4[:, j, 0:T], M1[:, j * TT:j * TT + T], vec[:, V_PS, j:j + 1], None,
                                          ALU.mult).then_inc(*give(dve, i, "od", 1))
                    dve.wait_ge(s["z"], nth("z", i, 2))
                    absolute(i, 4, X1, X3)
                if lv == 1:
                    log_sigmoid(i, 4, X1, X3)
                if lv == 2:
                    gate(i, 1, 3)
                if lv == 3:
                    mix_lo(i, 1)
                if lv == 4:
                    dve.wait_ge(s["z"], nth("z", i, 3))
                    absolute(i, 5, X1, X3)
                if lv == 5:
                    log_sigmoid(i, 5, X1, X3)
                    normalise(i, 0)
                if lv == 6:
                    gate(i, 2, 4)
                if lv == 7:
                    mix_lo(i, 2)
            query(i, 1)
            states(i, 1)
            dve.wait_ge(s["z"], nth("z", i, 4))
            absolute(i, 6, X1, X3)
            log_sigmoid(i, 6, X1, X3)
            normalise(i, 1)
            gate(i, 3, 5)
            mix_lo(i, 3)

        def dve_out(i):
            first, T, NC, C = dims(i)
            k = 2 // NC
            for c in range(NC):
                dve.wait_ge(s["yr"], nth("yr", i, k * (c + 1)))
                dve.wait_ge(*own(dve, i))
                dve.scalar_tensor_tensor(op[0:C, :], op[0:C, :], sy[0:C, c:c + 1], gpost[0:C, :], ALU.mult,
                                         ALU.mult).then_inc(*give(dve, i, "yg", k))
                dve.wait_ge(s["yg"], nth("yg", i, k * (c + 1)))
                dve.wait_ge(s["xre"], nth("xre", i, 16 * k * (c + 1)))
                dve.wait_ge(*own(dve, i))
                dve.tensor_tensor(xbuf[0:C, :], op[0:C, :], xbuf[0:C, :], ALU.add).then_inc(*give(dve, i, "yo", k))

        sc_count = dve.alloc_register("sc_count")

        @block.vector
        def _(_dve):
            i = 0
            dve.memset(cst[:, 0:1], EPS).then_inc(*give1(dve, "cstd"))
            dve.wait_ge(once["const0"], 16 * 3)
            dve.wait_ge(once["lrw"], 16)
            lr = B[:, 0, 0:KD * RANK].rearrange("p (k n) -> p k n", k=KD)
            dve.wait_ge(*own(dve, i))
            dve.tensor_tensor(lr, lr, gpre[:, :].unsqueeze(2).broadcast_to([128, KD, RANK]),
                              ALU.mult).then_inc(*give1(dve, "wlr"))
            dve.wait_ge(once["wlrh"], 1)
            dve.wait_ge(*own(dve, i))
            dve.scalar_tensor_tensor(w_lr[:, :, RANK:2 * RANK], lr, SW, w_lr[:, :, 0:RANK], ALU.mult,
                                     ALU.subtract).then_inc(*give1(dve, "wlr"))
            for n in range(len(ORDER)):
                dve.wait_ge(once["whi"], n + 1)
                dve.wait_ge(*own(dve, i))
                dve.scalar_tensor_tensor(w_lo[:, :, GW * n:GW * n + GW], stage[n % 2], SW, w_hi[:, :, GW * n:GW * n + GW],
                                         ALU.mult, ALU.subtract).then_inc(*give1(dve, "wlo"))
            dve.wait_ge(once["const"], 16 * N_CONST)
            for dst, src in zip((masks[:, :], masks0[:, :], keep[:, :], keep0[:, :]), mask_f):
                dve.tensor_copy(dst, src).then_inc(*give1(dve, "msk"))
            dve.wait_ge(once["const0"], 16 * 3)
            dve.tensor_copy(eye[:, :], ident[:, :]).then_inc(*give1(dve, "msk"))
            dve.wait_ge(*own(dve, i))
            dve.tensor_scalar(gpost[:, :], gpost[:, :], OS, None, ALU.mult).then_inc(*give1(dve, "cstd"))
            dve.wait_ge(once["cstd"], 2)
            dve_tile(0)
            dve.wait_ge(once["sdec"], 8)
            for b in range(DB):
                if b >= 2:
                    dve.wait_ge(once["su"], b - 1)
                V = (X1, X2)[b % 2][0:T0, :, :].rearrange("p j t -> p (j t)")[:, 0:2 * GW]
                dve.wait_ge(*own(dve, i))
                dve.tensor_scalar(V, VI[0:T0, 0, :], seqm[:, b + 1:b + 2], None, ALU.mult).then_inc(*give1(dve, "vm"))
                dve.wait_ge(once["su"], b + 1)
                for br in range(2):
                    for hh in range(2):
                        Sv = half(SS[br], hh)[:, b, :, 64 * hh:64 * hh + 64]
                        dve.wait_ge(*own(dve, i))
                        dve.tensor_tensor(Sv, Sv, half(M1, hh)[:, 256 * br:256 * br + 256].rearrange(
                            "p (j v) -> p j v", j=2)[:, :, 64 * hh:64 * hh + 64], ALU.add).then_inc(*give1(dve, "sv"))
            for k in range(KD):
                dve.wait_ge(once["wohi"], k + 1)
                if k == 0:
                    dve.wait_ge(once["sout"], 16 * 11)
                dve.wait_ge(*own(dve, i))
                dve.scalar_tensor_tensor(wo_lo[:, k, :], xbuf[:, :], SW, wo_hi[:, k, :], ALU.mult,
                                         ALU.subtract).then_inc(*give1(dve, "wolo"))
            dve_out(0)
            dve.reg_mov(sc_count, SIGNALS["sc"])
            with dve.Fori(1, NT + 1) as i:
                dve_tile(i)
                dve_out(i)


_INS = ("x_prompt", "x_sample", "state_gla", "state_conv", "state_hgrn", "state_pool", "meta_tokens", "norm_post", "w_in", "gla_w_a2", "pool_w", "w_out")
_OUTS = (("y_prompt", (SEQ, D), (1, SEQ, D)), ("y_sample", (DB, DS, D), (DB, DS, D)),
         ("gla_prompt", (4, HK, HK), (1, 1, 4, HK, HK)), ("conv_prompt", (2, GW), (1, 1, 2, GW)),
         ("hgrn_prompt", (4, HK, HK), (1, 1, 4, HK, HK)), ("pool_prompt", (POOLB, GW), (1, 1, POOLB, GW)),
         ("gla_sample", (DB, 4, HK, HK), (1, DB, 4, HK, HK)), ("conv_sample", (DB, 2, GW), (1, DB, 2, GW)),
         ("hgrn_sample", (DB, 4, HK, HK), (1, DB, 4, HK, HK)), ("pool_sample", (DB, POOLB, GW), (1, DB, POOLB, GW)))


def constants():
    import numpy as np
    p = np.arange(128)
    heads = (p[:, None] // HK == p[None, :] // HK)

    def level_mask(h, n, same):
        t = np.arange(n).reshape(-1, 2 * h)[:, h:].reshape(-1)
        q = np.arange(n)[:, None]
        return (q // (2 * h) == t // (2 * h)) & (q % (2 * h) < h) & same(q, t)

    masks = np.zeros((128, 8 * 64), np.float32)
    for lv, h in enumerate(LEVELS):
        masks[:, 64 * lv:64 * lv + 64] = level_mask(h, CH, lambda q, t: True)
    masks0 = np.zeros((T0, 4 * 24 + T0), np.float32)
    for n, h in enumerate(LEVELS[3:]):
        m = META if h >= 4 else T0
        masks0[:m, 24 * n:24 * n + m // 2] = level_mask(h, m, lambda q, t: True)
    masks0[:, 96:] = np.eye(T0)
    keep = np.ones((128, TT), np.float32)
    keep[:, ::CH] = 0
    keep0 = np.ones((128, T0), np.float32)
    keep0[:, 0] = 0
    keep0[:, META::DS] = 0
    rcnt = np.zeros((128, 2, META + 1), np.float32)
    for g, w in enumerate((2, 4, 8, 16)):
        r = rcnt[64 * (g % 2):64 * (g % 2) + 64, g // 2]
        r[:] = 1.0 / w
        r[:, :META] = (1.0 / np.minimum(np.arange(META) + 1, w)).astype(np.float32)
    seqm = np.zeros((T0, DB + 1), np.float32)
    seqm[:META, 0] = 1
    for b in range(DB):
        seqm[META + DS * b:META + DS * b + DS, b + 1] = 1
    return dict(c_ident=np.eye(128, dtype=np.float32), c_bones=heads.astype(np.float32), c_masks=masks,
                c_masks0=masks0, c_keep=keep, c_keep0=keep0,
                c_rcnt=rcnt, c_seqm=seqm)


def kernel(**inputs):
    import numpy as np
    import concourse.bacc as bacc
    from concourse.bass_utils import run_bass_kernel_spmd

    nc = bacc.Bacc("TRN2", target_bir_lowering=False, num_devices=1)
    arrays, aps = {}, {}

    def add(name, x):
        arrays["in_" + name] = x
        aps[name] = nc.dram_tensor("in_" + name, x.shape, mybir.dt.from_np(x.dtype), kind="ExternalInput").ap()

    for name in _INS:
        x = np.ascontiguousarray(inputs[name])
        if name not in ("x_sample", "meta_tokens"):
            x = x[0]
        add(name, x)
    add("norm_pre", np.ascontiguousarray(np.asarray(inputs["norm_pre"])[0].reshape(KD, 128).T))
    rows = [np.asarray(inputs[name])[0].reshape(-1, GW)
            for name in ("gla_b_a", "gla_norm", "hgrn_norm", "pool_scale", "conv_w")]
    add("vectors", np.ascontiguousarray(np.concatenate(rows).reshape(7, 2, 128).transpose(2, 0, 1)))
    for name, x in constants().items():
        add(name, x)
    outs = {name: nc.dram_tensor("out_" + name, shape, F32, kind="ExternalOutput").ap() for name, shape, _ in _OUTS}
    program(nc, aps, outs)
    r = run_bass_kernel_spmd(nc, [arrays], core_ids=[0]).results[0]
    return tuple(r["out_" + name].reshape(full) for name, _, full in _OUTS)
```

```python
from contextlib import ExitStack

import concourse.bass as bass
from concourse import mybir

F32 = mybir.dt.float32
F16 = mybir.dt.float16
BF16 = mybir.dt.bfloat16
U8 = mybir.dt.uint8
ACT = mybir.ActivationFunctionType
ALU = mybir.AluOpType

D = 1024
KD = D // 128
GW = 256
HK = 64
RANK = 16
SEQ = 2048
META = 16
DB, DS = 8, 4
T0 = META + DB * DS
TT = 256
CH = 128
NT = SEQ // TT
POOLB = 15
EPS = 1e-6
SH = 16.0
SW = 256.0
CS = 1.0 / (SH * SW)
OS = 1.0 / SW
LEVELS = (64, 32, 16, 8, 4, 2, 1)
NL = len(LEVELS) + 1
SCALE = (1.0 / 16.0, 1.0)

COL = dict(a_q=0, a_k=256, a_v=512, a_lr=768, a_z=784, b_b=1040, b_c=1296, b_v=1552, b_z=1808,
           c_q=2064, c_f=2320, c_i=2576, c_z=2832, d_v=3088, d_z=3344)
ORDER = ("a_q", "a_k", "a_v", "c_i", "c_f", "c_q", "b_c", "b_v", "b_b", "b_z", "d_v", "d_z", "a_z", "c_z")
AT = {g: n * GW for n, g in enumerate(ORDER)}
FILLS = ("lr", "a_q", "la", "a_k", "vi0", "vi1", "c_f", "c_q", "b_c", "b_v", "b_b", "b_z", "d_v", "d_z",
         "a_z", "c_z")
READER = dict(lr=("lr", 1), a_q=("q", 1), la=("la", 2), a_k=("k", 1), vi0=("vi", 1), vi1=("vi", 2),
              c_f=("cf", 1), c_q=("cq", 1), b_c=("bc", 1), b_v=("ub", 1), b_b=("bb", 1), b_z=("z", 1),
              d_v=("ud", 1), d_z=("z", 2), a_z=("z", 3), c_z=("z", 4))
NF = len(FILLS)
LB0 = 2 + META + DB * (2 + DS)
LD0 = 32 + DB * (POOLB + DS)
N_CONST = 14
N_ZERO = 11

SIGNALS = dict(
    xin=32,
    ssx=2, rln=2, rs=2,
    xn=2,
    xt=4,
    hhi=4, hlo=4,
    pj=NF,
    lr=1, q=1, k=1, vi=2, bc=1, ud=1, z=4,
    la=2, cf=1, cq=1, ub=1, bb=1,
    ab=7, ex=7, lg=7, ls=7, sg=5,
    kcs=1, kc=1, qc=1,
    bsc=2,
    gs=28, ge=14, gm=28,
    sc=2 * NL * 2,
    am=2 * NL * 2,
    eq=2, qt=2, dc=2,
    ks=2, ke=2, kh=2,
    kt=2, kte=2, up=2,
    st=16,
    o=4, sq=2, ns=2, nl=2, nr=2, on=4,
    hz=4,
    cv=6, wn=4, pd=4, po=1, od=2,
    gz=4, mg=4, mhi=4, mlo=4,
    yp=2, ss=2, yln=2, yr=2,
    yg=2, xre=32, yo=2, yst=32,
)


def program(nc, a, outs):
    ctx = ExitStack()
    with ctx:
        def sb(name, shape, dt=F32):
            return ctx.enter_context(nc.sbuf_tensor(name, shape, dt))

        def sem(name):
            return ctx.enter_context(nc.semaphore(name))

        w_hi = sb("w_hi", [128, KD, len(ORDER) * GW], F16)
        w_lo = sb("w_lo", [128, KD, len(ORDER) * GW], F16)
        w_lr = sb("w_lr", [128, KD, 2 * RANK], F16)
        wo_hi = sb("wo_hi", [128, KD, D], F16)
        wo_lo = sb("wo_lo", [128, KD, D], F16)
        h_hi = sb("h_hi", [128, KD, TT], F16)
        h_lo = sb("h_lo", [128, KD, TT], F16)
        m_hi = sb("m_hi", [128, KD, TT], F16)
        m_lo = sb("m_lo", [128, KD, TT], F16)
        xbuf = sb("xbuf", [128, D])
        gpost = sb("gpost", [128, D])
        G = [sb(f"G{n}", [128, 2, TT]) for n in range(2)]
        A = [sb(f"A{n}", [128, 4, CH]) for n in range(2)]
        VI = sb("VI", [128, 2, 2 * GW])
        S = [[sb(f"S{br}{n}", [128, 2, 128]) for n in range(2)] for br in range(2)]
        Q = [sb(f"Q{br}", [128, 2, TT]) for br in range(2)]
        K = [sb(f"K{br}", [128, 2, TT]) for br in range(2)]
        B = sb("B", [128, 2, TT])
        X1, X3, X4 = (sb(f"X{n}", [128, 2, TT + 16]) for n in (1, 3, 4))
        X2 = sb("X2", [128, 2, TT])
        ident = sb("ident", [128, 128])
        bones = sb("bones", [128, 128])
        masks = sb("masks", [128, 8 * 64], U8)
        eye = sb("eye", [128, CH], U8)
        masks0 = sb("masks0", [T0, 4 * 24 + T0], U8)
        keep = sb("keep", [128, TT], U8)
        keep0 = sb("keep0", [128, T0], U8)
        rcnt = sb("rcnt", [128, 2, META + 1])
        pw = sb("pw", [128, 2, 128])
        a2 = sb("a2", [2 * RANK, GW])
        seqm = sb("seqm", [T0, DB + 1])
        vec = sb("vec", [128, 7, 2])
        gpre = sb("gpre", [128, KD])
        cst = sb("cst", [128, 1])
        sx = sb("sx", [128, 2])
        sy = sb("sy", [128, 2])
        dec = sb("dec", [128, 2, 9])
        tailB = sb("tailB", [128, 2, 2])
        tailD = sb("tailD", [128, 2, POOLB])
        TD = K[0][:, :, 64:64 + DB * POOLB].rearrange("p j (b w) -> p j b w", b=DB)
        TB = K[0][:, :, 192:192 + DB * 2].rearrange("p j (b w) -> p j b w", b=DB)
        tl = K[1][:, :, 64:112]
        mask_f = [Q[0][:, :, :].rearrange("p j t -> p (j t)"), K[0][0:T0, 0, 0:4 * 24 + T0],
                  K[1][:, 0, 0:TT], K[1][:, 1, 0:T0]]
        KTS = [Q[n][:, :, 64:192] for n in range(2)]
        X5 = X3[:, :, :].rearrange("p j t -> p (j t)")

        def ps(name):
            return ctx.enter_context(nc.psum_tensor(name, [128, 512], F32))

        pj = [ps("pj0"), ps("pj1")]
        SC = [ps("sc0"), ps("sc1")]
        M0, M1 = ps("m0"), ps("m1")
        op = ctx.enter_context(nc.psum_tensor("op", [128, D], F32))

        s = {n: sem("s_" + n) for n in SIGNALS}
        once = {n: sem("o_" + n) for n in (
            "const0", "const", "wld0", "wld1", "wld2", "wld3", "wld4", "wld5", "wmul", "wmud", "wold0", "wold1", "wold2", "wold3", "wold4", "wold5", "whi", "wlo", "lrw", "wlr", "wohi", "wolo", "zero", "cstd",
            "tin", "tT", "wlrh", "tcp", "smp", "sdec", "vm", "su", "sv", "sout", "tl", "lT", "lcp", "fin", "pd0", "pp", "msk", "aa", "dd")}

        stage = [t.rearrange("p k n -> p (k n)").bitcast(F32).rearrange("p (k n) -> p k n", k=4)
                 for t in (wo_hi[:, 0:2, :], wo_hi[:, 2:4, :], wo_hi[:, 4:6, :], wo_hi[:, 6:8, :], m_hi[:, :, :])]
        stage.append(VI[:, :, :].rearrange("p c n -> p (c n)").rearrange("p (k n) -> p k n", k=4))
        NU = 2 * len(ORDER)
        wo_stage = [xbuf[:, 0:512], xbuf[:, 512:D], VI[:, 0, :], VI[:, 1, :]]
        wo_stage += [t[:, :, :].rearrange("p j t -> p (j t)") for t in (Q[1], K[1])]
        SS = [wo_lo[:, 4 * br:4 * br + 4, :].rearrange("p k n -> p (k n)").bitcast(F32)
              .rearrange("p (b j v) -> p b j v", b=DB, j=2) for br in range(2)]
        tin = m_lo[:, :, :].rearrange("p k n -> p (k n)").bitcast(F32)
        junk = X4[:, :, :].rearrange("p j t -> p (j t)")[:, 0:D // 2].bitcast(BF16)

        def nth(name, i, k):
            v = i * SIGNALS[name] + k
            assert not isinstance(v, int) or v > 0, (name, i, k)
            return v

        given, last = {}, {}

        def give(eng, i, name, n):
            given[name] = given.get(name, 0) + n
            last[eng.engine] = (s[name], name, i, given[name])
            return s[name], n

        def give1(eng, name):
            given["o_" + name] = given.get("o_" + name, 0) + 1
            last[eng.engine] = (once[name], None, 0, given["o_" + name])
            return once[name], 1

        def own(eng, i):
            which, name, tile, n = last[eng.engine]
            return which, (nth(name, tile, n) if name else n)

        def fresh(names):
            for name in names.split():
                assert given.get(name, SIGNALS[name]) == SIGNALS[name], name
                given[name] = 0

        def begin(eng, i, names, end):
            fresh(names)
            if not (isinstance(i, int) and i < 2):
                last[eng.engine] = (s[end], end, i, 0)

        block = ctx.enter_context(nc.Block())
        dve, act, pool, pe = nc.vector, nc.scalar, nc.gpsimd, nc.tensor
        VB_A, V_GA, V_PS, V_CW = 0, 1, 3, 4

        def dims(i):
            first = isinstance(i, int) and i == 0
            return first, (T0 if first else TT), (1 if first else 2), (T0 if first else CH)


        def half(t, hh):
            return t[64 * hh:64 * hh + 64]

        def seqs(t, at, n, w, lo, hi):
            return t[:, :, at:at + n * w].rearrange("p j (b w) -> p j b w", w=w)[:, :, :, lo:hi]

        def split(t, i, lv):
            h = LEVELS[lv]
            first, T, NC, C = dims(i)
            if first:
                n = META if h >= 4 else T0
                return t[:, :, 0:n].rearrange("p j (b w) -> p j b w", w=2 * h), n
            return t[:, :, :].rearrange("p j (b w) -> p (j b) w", w=2 * h), T

        def scaled(br, lv):
            return (G[0], X2, G[1])[lv % 3] if br else G[lv % 2]

        def levels(i):
            return [lv for lv in range(NL - 1) if not (isinstance(i, int) and i == 0 and LEVELS[lv] > META // 2)]

        def load_x(sp, i):
            first, T, NC, C = dims(i)
            if first:
                sp.dma_start(xbuf[0:META, :], a["meta_tokens"]).then_inc(s["xin"], 16)
                sp.dma_start(xbuf[META:T0, :], a["x_sample"].rearrange("b t d -> (b t) d")).then_inc(s["xin"], 16)
                return
            for c in range(2):
                if c == 0 and isinstance(i, int) and i == 1:
                    sp.wait_ge(s["xt"], nth("xt", 0, 4))
                elif c == 0:
                    sp.wait_ge(s["yst"], nth("yst", i - 2, 32))
                else:
                    sp.wait_ge(s["xt"], nth("xt", i, 2))
                sp.dma_start(xbuf[:, :], a["x_prompt"][bass.ds((i - 1) * TT + c * CH, CH), :]).then_inc(s["xin"], 16)

        def finish(sp, i):
            first, T, NC, C = dims(i)
            if first:
                sp.wait_ge(once["wolo"], 2 * KD)
                sp.dma_start(xbuf[0:META, :], a["meta_tokens"]).then_inc(s["xre"], 16)
                sp.dma_start(xbuf[META:T0, :], a["x_sample"].rearrange("b t d -> (b t) d")).then_inc(s["xre"], 16)
                sp.wait_ge(s["yo"], nth("yo", i, 2))
                for n in range(2):
                    sp.dma_start(outs["y_sample"].rearrange("b t d -> (b t) d")[16 * n:16 * n + 16, :],
                                 xbuf[META + 16 * n:META + 16 * n + 16, :]).then_inc(s["yst"], 16)
                return
            for c in range(2):
                if c == 0 and not (isinstance(i, int) and i == NT):
                    sp.wait_ge(s["xt"], nth("xt", i + 1, 4))
                elif c == 0:
                    sp.wait_ge(s["yst"], nth("yst", i, 0))
                else:
                    sp.wait_ge(s["yst"], nth("yst", i, 16))
                src = bass.ds((i - 1) * TT + c * CH, CH)
                sp.dma_start(xbuf[:, :], a["x_prompt"][src, :]).then_inc(s["xre"], 16)
                sp.wait_ge(s["yo"], nth("yo", i, c + 1))
                sp.dma_start(outs["y_prompt"][src, :], xbuf[:, :]).then_inc(s["yst"], 16)

        @block.sync
        def _(sp):
            load_x(sp, 0)
            n_const = 0

            def const(dst, src):
                nonlocal n_const
                sp.dma_start(dst, src).then_inc(once["const"], 16)
                n_const += 1

            sp.dma_start(ident[:, :], a["c_ident"]).then_inc(once["const0"], 16)
            sp.dma_start(bones[:, :], a["c_bones"]).then_inc(once["const0"], 16)
            sp.dma_start(gpre[:, :], a["norm_pre"]).then_inc(once["const0"], 16)
            w_src = a["w_in"].rearrange("(k p) n -> p k n", p=128)
            sp.dma_start(B[:, 0, 0:KD * RANK].rearrange("p (k n) -> p k n", k=KD),
                         w_src[:, :, COL["a_lr"]:COL["a_lr"] + RANK]).then_inc(once["lrw"], 16)

            def unit(u):
                if u >= len(stage):
                    sp.wait_ge(once["whi"], u - len(stage) + 1)
                    sp.wait_ge(once["wlo"], u - len(stage) + 1)
                g, k = COL[ORDER[u // 2]], 4 * (u % 2)
                sp.dma_start(stage[u % len(stage)], w_src[:, k:k + 4, g:g + GW]).then_inc(once["wld%d" % (u % len(stage))], 16)

            for u in range(len(stage)):
                unit(u)
            sp.dma_start(tin[0:DB * POOLB, 0:GW], a["state_pool"].rearrange("b t c -> (b t) c")).then_inc(once["tin"], 16)
            sp.dma_start(tin[0:DB * 2, GW:2 * GW], a["state_conv"].rearrange("b t c -> (b t) c")).then_inc(once["tin"], 16)
            for dst, name in ((mask_f[0], "c_masks"), (mask_f[1], "c_masks0"), (mask_f[2], "c_keep"), (mask_f[3], "c_keep0"),
                              (rcnt[:, :, :], "c_rcnt"), (seqm[:, :], "c_seqm"),
                              (a2[0:RANK, :], "gla_w_a2"), (a2[RANK:2 * RANK, :], "gla_w_a2")):
                const(dst, a[name])
            const(vec[:, :, :], a["vectors"])
            const(gpost[:, :], a["norm_post"].unsqueeze(0).broadcast_to([128, D]))
            sp.wait_ge(once["zero"], N_ZERO)
            for g in range(4):
                const(pw[64 * (g % 2):64 * (g % 2) + 64, g // 2, 64 * (g % 2):64 * (g % 2) + 64], a["pool_w"][g])
            assert n_const == N_CONST
            for br, name in enumerate(("state_gla", "state_hgrn")):
                for hh in range(2):
                    for j in range(2):
                        sp.dma_start(half(SS[br], hh)[:, :, j, 64 * hh:64 * hh + 64],
                                     a[name][:, 2 * j + hh, :, :].rearrange("b k v -> k b v")
                                     ).then_inc(once["smp"], 16)
            for u in range(len(stage), NU):
                unit(u)
            sp.dma_start(outs["pool_sample"][:, 0:POOLB - DS, :], a["state_pool"][:, DS:POOLB, :]).then_inc(once["sout"], 16)
            load_x(sp, 1)
            sp.wait_ge(once["lcp"], 2)
            sp.dma_start(outs["conv_sample"].rearrange("b t c -> (b t) c"), X5[0:DB * 2, 0:GW]).then_inc(once["sout"], 16)
            sp.dma_start(outs["pool_sample"][:, POOLB - DS:POOLB, :], X5[0:DB * DS, GW:2 * GW]).then_inc(once["sout"], 16)
            sp.wait_ge(once["sv"], 4 * DB)
            for br, name in enumerate(("gla_sample", "hgrn_sample")):
                for hh in range(2):
                    for j in range(2):
                        sp.dma_start(outs[name][:, 2 * j + hh, :, :].rearrange("b k v -> k b v"),
                                     half(SS[br], hh)[:, :, j, 64 * hh:64 * hh + 64]).then_inc(once["sout"], 16)
            sp.wait_ge(s["xt"], nth("xt", 1, 4))
            sp.wait_ge(once["su"], DB)
            sp.wait_ge(once["lT"], 2)
            for u in range(2 * KD):
                n, k, at = u % len(wo_stage), u // 2, 512 * (u % 2)
                if u >= len(wo_stage):
                    sp.wait_ge(once["wohi"], u - len(wo_stage) + 1)
                    sp.wait_ge(once["wolo"], u - len(wo_stage) + 1)
                sp.dma_start(wo_stage[n], a["w_out"][128 * k:128 * k + 128, at:at + 512]).then_inc(once["wold%d" % n], 16)
            finish(sp, 0)
            load_x(sp, 2)
            with sp.Fori(2, NT) as i:
                finish(sp, i - 1)
                load_x(sp, i + 1)
            finish(sp, NT - 1)
            finish(sp, NT)
            sp.wait_ge(s["st"], nth("st", NT, 16))
            for br, name in enumerate(("gla_prompt", "hgrn_prompt")):
                for hh in range(2):
                    for j in range(2):
                        sp.dma_start(outs[name][2 * j + hh, :, :],
                                     half(S[br][0], hh)[:, j, 64 * hh:64 * hh + 64]).then_inc(once["fin"], 16)
            sp.wait_ge(once["lcp"], 4)
            sp.dma_start(outs["conv_prompt"], X5[0:2, 0:GW]).then_inc(once["fin"], 16)
            sp.dma_start(outs["pool_prompt"], X5[0:POOLB, GW:2 * GW]).then_inc(once["fin"], 16)
            sp.wait_ge(s["yst"], 32 * (NT + 1))
            sp.wait_ge(once["sout"], 16 * 11)
            sp.wait_ge(once["fin"], 16 * 10)

        def level_parts(i, br, lv):
            first, T, NC, C = dims(i)
            h = LEVELS[lv]
            pre = (slice(None),) * (3 if first else 2)
            L, R = pre + (slice(0, h),), pre + (slice(h, 2 * h),)
            Gv, Bv, Qv, Kv = (split(x, i, lv)[0] for x in (scaled(br, lv), B, Q[br], K[br]))
            return Gv, Bv, Qv, Kv, L, R, pre + (slice(h - 1, h),)

        def pool_exponents(i, br, lv):
            first, T, NC, C = dims(i)
            todo = levels(i)
            Gv, Bv, Qv, Kv, L, R, M = level_parts(i, br, lv)
            mid = Bv[M].broadcast_to(list(Bv[L].shape))
            if lv == todo[0]:
                pool.wait_ge(s["bsc"], nth("bsc", i, br + 1))
            before = lv - (3 if br else 2)
            if before < todo[0]:
                if scaled(br, lv) is G[1] and (not first or br):
                    pool.wait_ge(s["up"], nth("up", i, br))
                    pool.wait_ge(s["qt"], nth("qt", i, br))
            else:
                pool.wait_ge(s["sc"], nth("sc", i, 2 * NL * br + 2 * (before + 1)))
            skip = (2 * todo[0]) if lv == todo[0] else 0
            pool.wait_ge(*own(pool, i))
            pool.tensor_tensor(Gv[R], Bv[R], mid, ALU.subtract).then_inc(*give(pool, i, "gs", 1 + skip))
            pool.wait_ge(*own(pool, i))
            pool.tensor_tensor(Gv[L], mid, Bv[L], ALU.subtract).then_inc(*give(pool, i, "gs", 1))

        def pool_scale(i, br, lv):
            todo = levels(i)
            Gv, Bv, Qv, Kv, L, R, M = level_parts(i, br, lv)
            pool.wait_ge(s["ge"], nth("ge", i, 7 * br + lv + 1))
            if lv == todo[0]:
                if br == 0:
                    pool.wait_ge(s["q"], nth("q", i, 1))
                    pool.wait_ge(s["k"], nth("k", i, 1))
                else:
                    pool.wait_ge(s["qc"], nth("qc", i, 1))
                    pool.wait_ge(s["kc"], nth("kc", i, 1))
            skip = (2 * todo[0]) if lv == todo[0] else 0
            pool.wait_ge(*own(pool, i))
            pool.tensor_tensor(Gv[R], Gv[R], Qv[R], ALU.mult).then_inc(*give(pool, i, "gm", 1 + skip))
            pool.wait_ge(*own(pool, i))
            pool.tensor_tensor(Gv[L], Gv[L], Kv[L], ALU.mult).then_inc(*give(pool, i, "gm", 1))

        def pool_levels(i, br):
            todo = levels(i)
            pool_exponents(i, br, todo[0])
            pool_scale(i, br, todo[0])
            pool_exponents(i, br, todo[1])
            for lv in todo[1:]:
                if lv + 1 < NL - 1:
                    pool_exponents(i, br, lv + 1)
                pool_scale(i, br, lv)

        def pool_key(i, br):
            first, T, NC, C = dims(i)
            g = G[0]
            pool.wait_ge(s["sc"], nth("sc", i, 2 * NL * br + 14))
            if first:
                pool.wait_ge(*own(pool, i))
                pool.tensor_tensor(g[:, :, 0:META], B[:, :, META - 1:META].broadcast_to([128, 2, META]),
                                   B[:, :, 0:META], ALU.subtract).then_inc(*give1(pool, "pp"))
                new = seqs(B, META, DB, DS, 0, DS)
                pool.wait_ge(*own(pool, i))
                pool.tensor_tensor(seqs(g, META, DB, DS, 0, DS), new[:, :, :, DS - 1:DS].broadcast_to([128, 2, DB, DS]),
                                   new, ALU.subtract).then_inc(*give(pool, i, "ks", 1))
            else:
                Bc = B[:, :, :].rearrange("p j (c t) -> p (j c) t", c=2)
                pool.wait_ge(*own(pool, i))
                pool.tensor_tensor(g[:, :, :].rearrange("p j (c t) -> p (j c) t", c=2),
                                   Bc[:, :, CH - 1:CH].broadcast_to([128, 4, CH]), Bc, ALU.subtract).then_inc(*give(pool, i, "ks", 1))
            pool.wait_ge(s["ke"], nth("ke", i, br + 1))
            pool.wait_ge(s["sc"], nth("sc", i, 2 * NL * (br + 1)))
            pool.wait_ge(*own(pool, i))
            pool.tensor_tensor(K[br][:, :, 0:T], K[br][:, :, 0:T], g[:, :, 0:T], ALU.mult).then_inc(*give(pool, i, "kh", 1))

        def times_norm(eng, u, name):
            w, k = stage[u % len(stage)], 4 * (u % 2)
            eng.wait_ge(once["wld%d" % (u % len(stage))], 16 * (u // len(stage) + 1))
            eng.wait_ge(*own(eng, 0))
            eng.tensor_tensor(w, w, gpre[:, k:k + 4].unsqueeze(2).broadcast_to([128, 4, GW]),
                              ALU.mult).then_inc(*give1(eng, name))

        def pool_tile(i):
            begin(pool, i, 'gs gm ks kh', 'kh')
            for br in range(2):
                pool_levels(i, br)
                pool_key(i, br)

        @block.gpsimd
        def _(_pool):
            i = 0
            for n, t in enumerate((A[0], A[1], S[0][0], S[0][1], S[1][0], S[1][1], pw, SS[0], SS[1], X3, X4)):
                pool.memset(t[:], 0.0).then_inc(*give1(pool, "zero"))
            pool.wait_ge(once["const0"], 16 * 3)
            for u in range(0, NU, 2):
                times_norm(pool, u, "wmul")
            pool_tile(0)
            pool_tile(1)
            with pool.Fori(2, NT) as i:
                pool_tile(i)
            pool_tile(NT)

        def proj(i, f):
            first, T, NC, C = dims(i)
            name, bank = FILLS[f], pj[f % 2]
            who, cnt = READER[FILLS[(f - 2) % NF]]
            if not first or f >= 2:
                pe.wait_ge(s[who], nth(who, i, cnt if f >= 2 else cnt - SIGNALS[who]))
            if name == "lr":
                pe.wait_ge(s["hhi"], nth("hhi", i, 4))
                pe.wait_ge(s["hlo"], nth("hlo", i, 4))
                if first:
                    pe.wait_ge(once["wlr"], 2)
                for k in range(KD):
                    for n, h in enumerate((h_hi, h_lo)):
                        m = pe.matmul(bank[0:2 * RANK, 0:T], w_lr[:, k, :], h[:, k, 0:T],
                                      start=(k == 0 and n == 0), stop=(k == KD - 1 and n == 1))
            elif name == "la":
                pe.wait_ge(s["lr"], nth("lr", i, 1))
                if first:
                    pe.wait_ge(once["const"], 16 * N_CONST)
                for j in range(2):
                    m = pe.matmul(bank[:, j * T:(j + 1) * T], a2[:, 128 * j:128 * j + 128], X3[0:2 * RANK, 0, 0:T],
                                  start=True, stop=True)
            elif name in ("vi0", "vi1"):
                c = int(name[2])
                if first and c == 1:
                    m = pe.matmul(bank[0:32, 0:4], ident[:, 0:32], ident[:, 0:4], start=True, stop=True)
                    m.then_inc(s["pj"], 1)
                    return
                if first:
                    pe.wait_ge(once["whi"], 8)
                    pe.wait_ge(once["wlo"], 8)
                at = AT["a_v"]
                passes = ((h_hi, w_hi), (h_hi, w_lo), (h_lo, w_hi))
                for n, (h, w) in enumerate(passes):
                    for k in range(KD):
                        m = pe.matmul(bank[0:C, :], h[:, k, c * CH:c * CH + C], w[:, k, at:at + 2 * GW],
                                      start=(n == 0 and k == 0), stop=(n == 2 and k == KD - 1))
            else:
                at = AT[name]
                if first:
                    pe.wait_ge(once["whi"], 2 * (at // GW + 1))
                    pe.wait_ge(once["wlo"], 2 * (at // GW + 1))
                for j in range(2):
                    for n, (w, h) in enumerate(((w_hi, h_hi), (w_hi, h_lo), (w_lo, h_hi))):
                        for k in range(KD):
                            m = pe.matmul(bank[:, j * T:(j + 1) * T], w[:, k, at + 128 * j:at + 128 * j + 128],
                                          h[:, k, 0:T], start=(n == 0 and k == 0), stop=(n == 2 and k == KD - 1))
            m.then_inc(s["pj"], 1)

        def transpose_x(i, c):
            first, T, NC, C = dims(i)
            pe.wait_ge(s["xn"], nth("xn", i, (c + 1) * (2 // NC)))
            for half_ in range(2):
                if c == 1:
                    pe.wait_ge(s["hlo"], nth("hlo", i, half_ + 1))
                elif half_ == 0 and not (isinstance(i, int) and i < 2):
                    pe.wait_ge(s["yo"], nth("yo", i - 2, 2))
                for k in range(4):
                    m = pe.transpose(op[:, 512 * half_ + 128 * k:512 * half_ + 128 * k + C],
                                     xbuf[0:C, 128 * (4 * half_ + k):128 * (4 * half_ + k) + 128], ident[0:C, 0:C])
                m.then_inc(s["xt"], 2 // NC)

        def scores(i, br, lv):
            first, T, NC, C = dims(i)
            unit = 2 * NL * br + 2 * lv
            for hh in range(2):
                if lv not in levels(i) and lv < NL - 1:
                    continue
                before = 2 * NL * br if lv == levels(i)[0] else unit
                if not first or before:
                    pe.wait_ge(s["am"], nth("am", i, before - 2 + hh + 1))
                if lv < NL - 1:
                    if hh == 0:
                        pe.wait_ge(s["gm"], nth("gm", i, 14 * br + 2 * lv + 2))
                    h, g = LEVELS[lv], scaled(br, lv)
                    for c in range(NC):
                        for j in range(2):
                            if first:
                                n = META if h >= 4 else T0
                                L = half(g, hh)[:, j, 0:n]
                            else:
                                n = CH
                                L = half(g, hh)[:, j, c * CH:c * CH + CH]
                            R = L.rearrange("p (b w) -> p b w", w=2 * h)[:, :, h:2 * h]
                            at = (2 * c + j) * 64
                            out = SC[hh][0:n, at:at + n // 2].rearrange("p (b w) -> p b w", w=h)
                            m = pe.matmul(out, L, R, start=True, stop=True)
                else:
                    if hh == 0 and br == 0:
                        pe.wait_ge(s["q"], nth("q", i, 1))
                        pe.wait_ge(s["k"], nth("k", i, 1))
                    for c in range(NC):
                        for j in range(2):
                            at = (2 * c + j) * 128
                            m = pe.matmul(SC[hh][0:C, at:at + C], half(K[br], hh)[:, j, c * CH:c * CH + C],
                                          half(Q[br], hh)[:, j, c * CH:c * CH + C], start=True, stop=True)
                skip = 2 * levels(i)[0] if lv == levels(i)[0] and hh == 0 else 0
                m.then_inc(s["sc"], 1 + skip)

        def keys(i, br):
            first, T, NC, C = dims(i)
            pe.wait_ge(s["kh"], nth("kh", i, br + 1))
            if not first or br:
                pe.wait_ge(s["on"], nth("on", i, 2 * br))
            for c in range(NC):
                for j in range(2):
                    m = pe.transpose(M0[0:C, 128 * (2 * c + j):128 * (2 * c + j) + 128],
                                     K[br][:, j, c * CH:c * CH + C], ident[:, :])
            m.then_inc(s["kt"], 1)
            pe.wait_ge(s["kte"], nth("kte", i, br + 1))
            pe.wait_ge(s["vi"], nth("vi", i, 2))
            if not first or br:
                pe.wait_ge(s["nl"], nth("nl", i, br))
            KT = G[1][:, :, :].rearrange("p j t -> p (j t)")
            n = META if first else CH
            for c in range(NC):
                for j in range(2):
                    cj = 128 * (2 * c + j)
                    v = GW * br + 128 * j
                    m = pe.matmul(M1[:, cj:cj + 128], KT[0:n, cj:cj + 128], VI[0:n, c, v:v + 128], start=True, stop=True)
            m.then_inc(s["up"], 1)

        def outputs(i, br):
            first, T, NC, C = dims(i)
            pe.wait_ge(s["am"], nth("am", i, 2 * NL * (br + 1)))
            pe.wait_ge(s["qt"], nth("qt", i, br + 1))
            if first and br == 0:
                pe.wait_ge(once["smp"], 16 * 8)
            for c in range(NC):
                for j in range(2):
                    at = j * TT + c * CH
                    for hh in range(2):
                        v = GW * br + 128 * j + 64 * hh
                        pe.matmul(half(M0, hh)[:, at:at + C], VI[0:C, c, v:v + 64], A[hh][0:C, 2 * c + j, 0:C],
                                  start=True, stop=False, skip_group_check=True)
                    if first:
                        for b in range(DB):
                            t = META + DS * b
                            m = pe.matmul(M0[:, at + t:at + t + DS], SS[br][:, b, j, :], Q[br][:, j, t:t + DS],
                                          start=False, stop=True, skip_group_check=True)
                    else:
                        if j == 0:
                            pe.wait_ge(s["st"], nth("st", i, 8 * br + 4 * c))
                        m = pe.matmul(M0[:, at:at + C], S[br][c][:, j, :], Q[br][:, j, c * CH:c * CH + C],
                                      start=False, stop=True, skip_group_check=True)
                m.then_inc(s["o"], 2 // NC)

        def pool_product(i):
            first, T, NC, C = dims(i)
            pe.wait_ge(s["pd"], nth("pd", i, 4))
            pe.wait_ge(s["st"], nth("st", i, 8))
            for j in range(2):
                if first:
                    pe.matmul(M1[:, j * TT:j * TT + META], pw[:, j, :], X1[:, j, POOLB:POOLB + META],
                              start=True, stop=True)
                    new = seqs(X1, 32, DB, POOLB + DS, POOLB, POOLB + DS)[:, j]
                    m = pe.matmul(M1[:, j * TT + META:j * TT + T0].rearrange("p (b w) -> p b w", w=DS), pw[:, j, :],
                                  new, start=True, stop=True)
                else:
                    m = pe.matmul(M1[:, j * TT:j * TT + T], pw[:, j, :], X1[:, j, POOLB:POOLB + T], start=True, stop=True)
            m.then_inc(s["po"], 1)

        def head_sums(i, br):
            first, T, NC, C = dims(i)
            pe.wait_ge(s["sq"], nth("sq", i, br + 1))
            if br == 0:
                pe.wait_ge(s["od"], nth("od", i, 2))
            else:
                pe.wait_ge(s["st"], nth("st", i, 16))
            for j in range(2):
                m = pe.matmul(M1[:, j * TT:j * TT + T], bones[:, :], X4[:, j, 0:T], start=True, stop=True)
            m.then_inc(s["ns"], 1)

        def out_product(i, c):
            first, T, NC, C = dims(i)
            if c == 0:
                pe.wait_ge(s["mlo"], nth("mlo", i, 4))
                if first:
                    pe.wait_ge(once["wohi"], 2 * KD)
                    pe.wait_ge(once["wolo"], 2 * KD)
                if isinstance(i, int) and i == NT:
                    pe.wait_ge(s["yo"], nth("yo", i, 0))
                else:
                    pe.wait_ge(s["hlo"], nth("hlo", i + 1, 4))
            else:
                pe.wait_ge(s["yo"], nth("yo", i, 1))
            for n in range(2):
                for p, (x, w) in enumerate(((m_hi, wo_hi), (m_hi, wo_lo), (m_lo, wo_hi))):
                    for k in range(KD):
                        m = pe.matmul(op[0:C, 512 * n:512 * n + 512], x[:, k, c * CH:c * CH + C],
                                      w[:, k, 512 * n:512 * n + 512], start=(p == 0 and k == 0),
                                      stop=(p == 2 and k == KD - 1))
            m.then_inc(s["yp"], 2 // NC)

        def pe_tile(i):
            first = isinstance(i, int) and i == 0
            short = isinstance(i, int) and i == 1
            end = isinstance(i, int) and i == NT
            for f in (1, 2, 3):
                proj(i, f)
            if not first:
                out_product(i - 1, 0)
            for lv in range(NL):
                scores(i, 0, lv)
                if lv == 2:
                    if not first and not short:
                        out_product(i - 1, 1)
                else:
                    proj(i, 4 + lv - (lv > 2))
            proj(i, 11)
            keys(i, 0)
            proj(i, 12)
            outputs(i, 0)
            for lv in range(NL):
                scores(i, 1, lv)
                if lv == 0:
                    proj(i, 13)
                if lv == 3:
                    proj(i, 14)
                if lv == 4:
                    pool_product(i)
                if lv == 5:
                    proj(i, 15)
                if lv == 6 and not end:
                    transpose_x(i + 1, 0)
                if lv == 7:
                    head_sums(i, 0)
                    if not end:
                        transpose_x(i + 1, 1)
            keys(i, 1)
            if not end:
                proj(i + 1, 0)
            outputs(i, 1)
            head_sums(i, 1)

        def tails_in():
            pe.wait_ge(once["tin"], 32)
            pe.wait_ge(once["const0"], 16 * 3)
            for j in range(2):
                pe.transpose(M0[:, 128 * j:128 * j + DB * POOLB], tin[0:DB * POOLB, 128 * j:128 * j + 128],
                             ident[0:DB * POOLB, 0:DB * POOLB])
                m = pe.transpose(M0[:, GW + 128 * j:GW + 128 * j + DB * 2], tin[0:DB * 2, GW + 128 * j:GW + 128 * j + 128],
                                 ident[0:DB * 2, 0:DB * 2])
            m.then_inc(once["tT"], 1)

        def tail_out(n, t, cols, at):
            for j in range(2):
                m = pe.transpose(M0[0:cols, at + 128 * j:at + 128 * j + 128], t[:, j, 0:cols], ident[:, :])
            m.then_inc(once["lT"], 1)

        @block.tensor
        def _(_pe):
            transpose_x(0, 0)
            tails_in()
            pe.wait_ge(once["tcp"], 2)
            proj(0, 0)
            pe_tile(0)
            pe.wait_ge(s["on"], nth("on", 0, 4))
            pe.wait_ge(once["tl"], 2)
            tail_out(0, tl, DB * 2, 0)
            tail_out(1, tl[:, :, 16:], DB * DS, GW)
            for b in range(DB):
                pe.wait_ge(once["vm"], b + 1)
                if b == 0:
                    pe.wait_ge(s["hlo"], nth("hlo", 1, 4))
                if b >= 2:
                    pe.wait_ge(once["sv"], 4 * (b - 1))
                for br in range(2):
                    KTb = KTS[br]
                    for j in range(2):
                        m = pe.matmul(op[:, 512 * (b % 2) + 128 * (2 * br + j):512 * (b % 2) + 128 * (2 * br + j) + 128], KTb[0:T0, j, :],
                                      (X1, X2)[b % 2][0:T0, :, :].rearrange("p j t -> p (j t)")[:, GW * br + 128 * j:
                                      GW * br + 128 * j + 128], start=True, stop=True)
                m.then_inc(once["su"], 1)
            pe_tile(1)
            with pe.Fori(2, NT) as i:
                pe_tile(i)
            pe_tile(NT)
            out_product(NT, 0)
            out_product(NT, 1)
            pe.wait_ge(s["on"], nth("on", NT, 4))
            pe.wait_ge(once["lcp"], 2)
            tail_out(2, tailB, 2, 0)
            tail_out(3, tailD, POOLB, GW)

        def evac(i, f, out, name, scale=CS):
            first, T, NC, C = dims(i)
            act.wait_ge(s["pj"], nth("pj", i, f + 1))
            act.wait_ge(*own(act, i))
            act.activation(out, pj[f % 2][:, 0:2 * T].rearrange("p (j t) -> p j t", j=2), ACT.Copy,
                           scale=scale).then_inc(*give(act, i, name, 1))

        def log_gate(i, n, E):
            first, T, NC, C = dims(i)
            act.wait_ge(s["ab"], nth("ab", i, n + 1))
            act.wait_ge(*own(act, i))
            act.activation(E[:, :, 0:T], E[:, :, 0:T], ACT.Exp, scale=-1.0).then_inc(*give(act, i, "ex", 1))
            act.wait_ge(s["ex"], nth("ex", i, n + 1))
            act.wait_ge(*own(act, i))
            act.activation(E[:, :, 0:T], E[:, :, 0:T], ACT.Ln, bias=1.0).then_inc(*give(act, i, "lg", 1))

        def sigmoid(i, n, E):
            first, T, NC, C = dims(i)
            act.wait_ge(s["ls"], nth("ls", i, n + 1))
            act.wait_ge(*own(act, i))
            act.activation(E[:, :, 0:T], E[:, :, 0:T], ACT.Exp).then_inc(*give(act, i, "sg", 1))

        def level_exp(i, br, lv):
            if lv not in levels(i):
                return
            Gv, n = split(scaled(br, lv), i, lv)
            act.wait_ge(s["gs"], nth("gs", i, 14 * br + 2 * lv + 2))
            g = scaled(br, lv)[:, :, 0:n]
            skip = lv if lv == levels(i)[0] else 0
            act.wait_ge(*own(act, i))
            act.activation(g, g, ACT.Exp, scale=SCALE[br]).then_inc(*give(act, i, "ge", 1 + skip))

        def decays(i, br):
            first, T, NC, C = dims(i)
            act.wait_ge(s["sc"], nth("sc", i, 2 * NL * br + 12))
            act.wait_ge(*own(act, i))
            act.activation(G[1][:, :, 0:T], B[:, :, 0:T], ACT.Exp, scale=SCALE[br]).then_inc(*give(act, i, "eq", 1))
            ends = B[:, :, META - 1:T0:DS] if first else B[:, :, CH - 1:TT:CH]
            if not first:
                act.wait_ge(s["st"], nth("st", i, 8 * br))
            act.wait_ge(*own(act, i))
            act.activation(dec[:, :, 0:9 if first else 2], ends, ACT.Exp, scale=SCALE[br]).then_inc(*give(act, i, "dc", 1))
            act.wait_ge(s["ks"], nth("ks", i, br + 1))
            act.wait_ge(*own(act, i))
            act.activation(G[0][:, :, 0:T], G[0][:, :, 0:T], ACT.Exp, scale=SCALE[br]).then_inc(*give(act, i, "ke", 1))

        def keys_by_token(i, br):
            first, T, NC, C = dims(i)
            act.wait_ge(s["kt"], nth("kt", i, br + 1))
            act.wait_ge(s["qt"], nth("qt", i, br + 1))
            if first:
                act.wait_ge(*own(act, i))
                act.activation(KTS[br][0:T0, :, :], M0[0:T0, 0:256].rearrange("p (j n) -> p j n", j=2),
                               ACT.Copy).then_inc(*give1(act, "aa"))
                act.wait_ge(*own(act, i))
                act.activation(G[1][0:META, :, :].rearrange("p j t -> p (j t)")[:, 0:256], M0[0:META, 0:256],
                               ACT.Copy).then_inc(*give(act, i, "kte", 1))
            else:
                act.wait_ge(*own(act, i))
                act.activation(G[1][:, :, :].rearrange("p j t -> p (j t)"), M0[:, :], ACT.Copy).then_inc(*give(act, i, "kte", 1))

        def square(i, br):
            first, T, NC, C = dims(i)
            act.wait_ge(s["o"], nth("o", i, 2 * br + 2))
            act.wait_ge(s["mlo"], nth("mlo", i, 2 if br == 0 else 3))
            act.wait_ge(*own(act, i))
            act.activation(X4[:, :, 0:T], M0[:, :].rearrange("p (j t) -> p j t", j=2)[:, :, 0:T],
                           ACT.Square).then_inc(*give(act, i, "sq", 1))

        def inv_rms(i, br):
            first, T, NC, C = dims(i)
            act.wait_ge(s["ns"], nth("ns", i, br + 1))
            act.wait_ge(*own(act, i))
            act.activation(X4[:, :, 0:T], M1[:, :].rearrange("p (j t) -> p j t", j=2)[:, :, 0:T], ACT.Ln,
                           scale=1.0 / HK, bias=cst[:, 0:1]).then_inc(*give(act, i, "nl", 1))
            act.wait_ge(s["nl"], nth("nl", i, br + 1))
            act.wait_ge(*own(act, i))
            act.activation(X4[:, :, 0:T], X4[:, :, 0:T], ACT.Exp, scale=-0.5).then_inc(*give(act, i, "nr", 1))

        def mix_hi(i, n):
            first, T, NC, C = dims(i)
            at = (2, 6, 0, 4)[n]
            act.wait_ge(s["mg"], nth("mg", i, n + 1))
            if n == 0:
                if not first:
                    act.wait_ge(s["yp"], nth("yp", i, 0))
            act.wait_ge(*own(act, i))
            act.activation(m_hi[:, at:at + 2, 0:T], X4[:, :, 0:T], ACT.Copy).then_inc(*give(act, i, "mhi", 1))

        def x_norm(i, c):
            first, T, NC, C = dims(i)
            k = 2 // NC
            if c == 0:
                fresh("ssx rln rs hhi")
            act.wait_ge(s["xin"], nth("xin", i, 16 * (c + 1) * k))
            if c == 1:
                act.wait_ge(s["hlo"], nth("hlo", i, 2))
            elif not first:
                if not (isinstance(i, int) and i == 1):
                    act.wait_ge(s["yo"], nth("yo", i - 2, 2))
                act.wait_ge(s["xn"], nth("xn", i, 0))
            act.wait_ge(*own(act, i))
            act.activation(op[0:C, :], xbuf[0:C, :], ACT.Square, accum_out=sx[0:C, c:c + 1]).then_inc(*give(act, i, "ssx", k))
            act.wait_ge(s["ssx"], nth("ssx", i, k * (c + 1)))
            act.wait_ge(*own(act, i))
            act.activation(sx[0:C, c:c + 1], sx[0:C, c:c + 1], ACT.Ln, scale=1.0 / D,
                           bias=cst[0:C, 0:1]).then_inc(*give(act, i, "rln", k))
            act.wait_ge(s["rln"], nth("rln", i, k * (c + 1)))
            act.wait_ge(*own(act, i))
            act.activation(sx[0:C, c:c + 1], sx[0:C, c:c + 1], ACT.Exp, scale=-0.5).then_inc(*give(act, i, "rs", k))

        def x_hi(i, c):
            first, T, NC, C = dims(i)
            k = 2 // NC
            for n in range(2):
                act.wait_ge(s["xt"], nth("xt", i, k * (2 * c + n + 1) if not first else 2 * n + 2))
                if c == 0 and n == 0 and not first:
                    act.wait_ge(s["pj"], nth("pj", i, 0))
                act.wait_ge(*own(act, i))
                act.activation(h_hi[:, 4 * n:4 * n + 4, c * CH:c * CH + C],
                               op[:, 512 * n:512 * n + 512].rearrange("p (k t) -> p k t", k=4)[:, :, 0:C],
                               ACT.Copy).then_inc(*give(act, i, "hhi", k))

        def values(i, c):
            first, T, NC, C = dims(i)
            act.wait_ge(s["pj"], nth("pj", i, 5 + c))
            if isinstance(i, int) and i == 1:
                act.wait_ge(once["wolo"], 2 * KD)
            act.wait_ge(*own(act, i))
            if c >= NC:
                act.activation(VI[0:1, 1, 0:1], cst[0:1, 0:1], ACT.Copy).then_inc(*give(act, i, "vi", 1))
            else:
                act.activation(VI[0:C, c, :], pj[c % 2][0:C, :], ACT.Copy, scale=CS).then_inc(*give(act, i, "vi", 1))

        def pooling_values(i):
            first, T, NC, C = dims(i)
            act.wait_ge(s["gz"], nth("gz", i, 1))
            if not first:
                evac(i, 12, X3[:, :, POOLB:POOLB + T], "ud")
                return
            act.wait_ge(s["pj"], nth("pj", i, 13))
            act.wait_ge(*own(act, i))
            act.activation(X3[:, :, POOLB:POOLB + META],
                           pj[0][:, 0:2 * T].rearrange("p (j t) -> p j t", j=2)[:, :, 0:META], ACT.Copy,
                           scale=CS).then_inc(*give1(act, "aa"))
            for j in range(2):
                act.wait_ge(*own(act, i))
                m = act.activation(seqs(X3, 32, DB, POOLB + DS, POOLB, POOLB + DS)[:, j],
                                   pj[0][:, j * T + META:j * T + T0].rearrange("p (b w) -> p b w", w=DS), ACT.Copy,
                                   scale=CS)
            m.then_inc(*give(act, i, "ud", 1))

        def w_out_upper():
            act.wait_ge(once["whi"], NU)
            act.wait_ge(once["wlo"], NU)
            for u in range(2 * KD):
                n, k, at = u % len(wo_stage), u // 2, 512 * (u % 2)
                act.wait_ge(once["wold%d" % n], 16 * (u // len(wo_stage) + 1))
                act.wait_ge(*own(act, 0))
                act.activation(wo_hi[:, k, at:at + 512], wo_stage[n], ACT.Copy, scale=SW).then_inc(*give1(act, "wohi"))

        def act_tile(i):
            begin(act, i, 'lr q k vi bc ud z ex lg sg kc ge eq dc ke kte sq nl nr mhi', 'mhi')
            first, T, NC, C = dims(i)
            short = isinstance(i, int) and i == 1
            end = isinstance(i, int) and i == NT
            act.wait_ge(s["pj"], nth("pj", i, 1))
            if not first:
                act.wait_ge(s["gz"], nth("gz", i, 0))
            act.wait_ge(*own(act, i))
            act.activation(X3[0:2 * RANK, 0, 0:T], pj[0][0:2 * RANK, 0:T], ACT.Copy, scale=CS).then_inc(*give(act, i, "lr", 1))
            if not first:
                act.wait_ge(s["sc"], nth("sc", i, 0))
            if not first:
                act.wait_ge(s["o"], nth("o", i, 0))
            if first:
                act.wait_ge(once["msk"], 5)
            evac(i, 1, Q[0][:, :, 0:T], "q", CS * HK ** -0.5)
            evac(i, 3, K[0][:, :, 0:T], "k")
            log_gate(i, 0, X2)
            if first:
                for u in range(len(stage), NU):
                    upper(u)
            level_exp(i, 0, 0)
            level_exp(i, 0, 1)
            if short:
                w_out_upper()
            if not first:
                y_norm(i - 1, 0)
            values(i, 0)
            level_exp(i, 0, 2)
            values(i, 1)
            level_exp(i, 0, 3)
            if not first and not short:
                y_norm(i - 1, 1)
            level_exp(i, 0, 4)
            level_exp(i, 0, 5)
            log_gate(i, 1, X2)
            log_gate(i, 2, X3)
            act.wait_ge(s["kcs"], nth("kcs", i, 1))
            act.wait_ge(*own(act, i))
            act.activation(K[1][:, :, 0:T], X1[:, :, 0:T], ACT.Exp).then_inc(*give(act, i, "kc", 1))
            level_exp(i, 0, 6)
            sigmoid(i, 2, X3)
            act.wait_ge(s["qc"], nth("qc", i, 1))
            evac(i, 8, X3[:, :, 0:T], "bc")
            decays(i, 0)
            evac(i, 11, X1[:, :, 0:T], "z")
            keys_by_token(i, 0)
            level_exp(i, 1, 0)
            level_exp(i, 1, 1)
            log_gate(i, 3, X3)
            level_exp(i, 1, 2)
            sigmoid(i, 3, X3)
            mix_hi(i, 0)
            level_exp(i, 1, 3)
            pooling_values(i)
            level_exp(i, 1, 4)
            level_exp(i, 1, 5)
            act.wait_ge(s["po"], nth("po", i, 1))
            evac(i, 13, X1[:, :, 0:T], "z")
            level_exp(i, 1, 6)
            log_gate(i, 4, X3)
            if not end:
                x_norm(i + 1, 0)
            sigmoid(i, 4, X3)
            mix_hi(i, 1)
            if not end:
                x_hi(i + 1, 0)
            square(i, 0)
            decays(i, 1)
            if not end:
                x_norm(i + 1, 1)
            inv_rms(i, 0)
            act.wait_ge(s["mg"], nth("mg", i, 2))
            evac(i, 14, X1[:, :, 0:T], "z")
            log_gate(i, 5, X3)
            if not end:
                x_hi(i + 1, 1)
            keys_by_token(i, 1)
            sigmoid(i, 5, X3)
            mix_hi(i, 2)
            act.wait_ge(s["mg"], nth("mg", i, 3))
            evac(i, 15, X1[:, :, 0:T], "z")
            log_gate(i, 6, X3)
            square(i, 1)
            inv_rms(i, 1)
            sigmoid(i, 6, X3)
            mix_hi(i, 3)

        def y_norm(i, c):
            first, T, NC, C = dims(i)
            k = 2 // NC
            if c == 0:
                fresh("ss yln yr")
                act.wait_ge(s["mlo"], nth("mlo", i, 4))
            act.wait_ge(s["yp"], nth("yp", i, k * (c + 1)))
            act.wait_ge(*own(act, i))
            act.activation(junk[0:C, :], op[0:C, :], ACT.Square, scale=OS,
                           accum_out=sy[0:C, c:c + 1]).then_inc(*give(act, i, "ss", k))
            act.wait_ge(s["ss"], nth("ss", i, k * (c + 1)))
            act.wait_ge(*own(act, i))
            act.activation(sy[0:C, c:c + 1], sy[0:C, c:c + 1], ACT.Ln, scale=1.0 / D,
                           bias=cst[0:C, 0:1]).then_inc(*give(act, i, "yln", k))
            act.wait_ge(s["yln"], nth("yln", i, k * (c + 1)))
            act.wait_ge(*own(act, i))
            act.activation(sy[0:C, c:c + 1], sy[0:C, c:c + 1], ACT.Exp, scale=-0.5).then_inc(*give(act, i, "yr", k))

        def upper(u):
            n, k = u // 2, 4 * (u % 2)
            act.wait_ge(once["wmud" if u % 2 else "wmul"], n + 1)
            act.wait_ge(*own(act, 0))
            act.activation(w_hi[:, k:k + 4, GW * n:GW * n + GW], stage[u % len(stage)], ACT.Copy,
                           scale=SW).then_inc(*give1(act, "whi"))

        @block.scalar
        def _(_act):
            i = 0
            act.preload_act_table_set("natural_log_exp_and_others")
            act.wait_ge(once["cstd"], 1)
            act.wait_ge(once["lrw"], 16)
            act.wait_ge(once["wlr"], 1)
            act.activation(w_lr[:, :, 0:RANK], B[:, 0, 0:KD * RANK].rearrange("p (k n) -> p k n", k=KD), ACT.Copy,
                           scale=SW).then_inc(*give1(act, "wlrh"))
            x_norm(0, 0)
            x_hi(0, 0)
            for u in range(len(stage)):
                upper(u)
            act.wait_ge(once["tT"], 1)
            act.wait_ge(once["zero"], N_ZERO)
            act.wait_ge(once["msk"], 5)
            for j in range(2):
                act.wait_ge(*own(act, i))
                act.activation(TD[:, j, :, :], M0[:, 128 * j:128 * j + DB * POOLB].rearrange("p (b w) -> p b w", b=DB),
                               ACT.Copy).then_inc(*give1(act, "aa"))
                act.wait_ge(*own(act, i))
                act.activation(TB[:, j, :, :], M0[:, GW + 128 * j:GW + 128 * j + DB * 2].rearrange("p (b w) -> p b w", b=DB),
                               ACT.Copy).then_inc(*give1(act, "tcp"))
            act_tile(0)
            act.wait_ge(s["gz"], nth("gz", 0, 4))
            for n, rows in ((0, DB * 2), (1, DB * DS)):
                act.wait_ge(once["lT"], 2)
                act.wait_ge(*own(act, i))
                act.activation(X5[0:rows, GW * n:GW * n + GW], M0[0:rows, GW * n:GW * n + GW],
                               ACT.Copy).then_inc(*give1(act, "lcp"))
            act.wait_ge(once["sout"], 16 * 11)
            act_tile(1)
            with act.Fori(2, NT) as i:
                act_tile(i)
            act_tile(NT)
            y_norm(NT, 0)
            y_norm(NT, 1)
            for n, rows in ((0, 2), (1, POOLB)):
                act.wait_ge(once["lT"], 4)
                act.wait_ge(*own(act, i))
                act.activation(X5[0:rows, GW * n:GW * n + GW], M0[0:rows, GW * n:GW * n + GW],
                               ACT.Copy).then_inc(*give1(act, "lcp"))

        def absolute(i, n, z, E):
            first, T, NC, C = dims(i)
            dve.wait_ge(*own(dve, i))
            dve.scalar_tensor_tensor(E[:, :, 0:T], z[:, :, 0:T], -1.0, z[:, :, 0:T], ALU.mult, ALU.max).then_inc(*give(dve, i, "ab", 1))

        def log_sigmoid(i, n, z, E):
            first, T, NC, C = dims(i)
            dve.wait_ge(s["lg"], nth("lg", i, n + 1))
            dve.wait_ge(*own(dve, i))
            dve.scalar_tensor_tensor(E[:, :, 0:T], z[:, :, 0:T], 0.0, E[:, :, 0:T], ALU.min,
                                     ALU.subtract).then_inc(*give(dve, i, "ls", 1))

        def running_sum(i, br):
            first, T, NC, C = dims(i)
            dve.wait_ge(s["ls"], nth("ls", i, br + 1))
            if br == 0:
                if not first:
                    dve.wait_ge(s["kh"], nth("kh", i, 0))
                if not first:
                    dve.wait_ge(s["eq"], nth("eq", i, 0))
                if not first:
                    dve.wait_ge(s["dc"], nth("dc", i, 0))
            else:
                dve.wait_ge(s["ks"], nth("ks", i, 1))
                dve.wait_ge(s["eq"], nth("eq", i, 1))
                dve.wait_ge(s["dc"], nth("dc", i, 1))
            for j in range(2):
                dve.wait_ge(*own(dve, i))
                m = dve.tensor_tensor_scan(B[:, j, 0:T], (keep0 if first else keep)[:, :], X2[:, j, 0:T],
                                           0.0, ALU.mult, ALU.add)
            m.then_inc(*give(dve, i, "bsc", 1))

        def copy_scores(i, br, lv):
            first, T, NC, C = dims(i)
            if lv < NL - 1 and lv not in levels(i):
                return
            for hh in range(2):
                if first:
                    dve.wait_ge(s["sc"], nth("sc", i, 2 * NL * br + 2 * lv + hh + 1))
                else:
                    dve.reg_add(sc_count, sc_count, 1)
                    dve.wait_ge(once["cstd"], 2)
                    dve.wait_ge(s["sc"], sc_count)
                if lv == levels(i)[0] and hh == 0:
                    if not first:
                        dve.wait_ge(s["o"], nth("o", i, 2 * br))
                skip = 2 * lv if lv == levels(i)[0] and hh == 0 else 0
                if lv < NL - 1:
                    h = LEVELS[lv]
                    n = (META if h >= 4 else T0) if first else CH
                    q = 2 * NC
                    mk = masks0[0:n, 24 * (lv - 3):24 * (lv - 3) + n // 2] if first else masks[:, 64 * lv:64 * lv + 64]
                    mk = mk.rearrange("p (b w) -> p b w", w=h)
                    for cj in range(q):
                        out = A[hh][0:n, cj, 0:n].rearrange("p (b w) -> p b w", w=2 * h)[:, :, h:2 * h]
                        m = dve.copy_predicated(out, mk, SC[hh][0:n, 64 * cj:64 * cj + n // 2].rearrange(
                            "p (b w) -> p b w", w=h))
                else:
                    mk = masks0[0:T0, 96:96 + T0] if first else eye[:, :]
                    q = 2 * NC
                    m = dve.copy_predicated(A[hh][0:C, 0:q, 0:C], mk.unsqueeze(1).broadcast_to([C, q, C]),
                                            SC[hh][0:C, 0:128 * q].rearrange("p (q t) -> p q t", t=128)[:, :, 0:C])
                m.then_inc(*give(dve, i, "am", 1 + skip))

        def query(i, br):
            first, T, NC, C = dims(i)
            dve.wait_ge(s["eq"], nth("eq", i, br + 1))
            dve.wait_ge(s["gm"], nth("gm", i, 14 * br + 14))
            dve.wait_ge(*own(dve, i))
            dve.tensor_tensor(Q[br][:, :, 0:T], Q[br][:, :, 0:T], G[1][:, :, 0:T], ALU.mult).then_inc(*give(dve, i, "qt", 1))

        def states(i, br, c):
            first, T, NC, C = dims(i)
            if first and c == 1:
                return
            dve.wait_ge(s["up"], nth("up", i, br + 1))
            dve.wait_ge(s["dc"], nth("dc", i, br + 1))
            if first:
                for hh in range(2):
                    dve.wait_ge(*own(dve, i))
                    dve.tensor_copy(half(S[br][0], hh)[:, :, 64 * hh:64 * hh + 64],
                                    half(M1, hh)[:, 0:256].rearrange("p (j v) -> p j v", j=2)[:, :, 64 * hh:64 * hh + 64]
                                    ).then_inc(*give(dve, i, "st", 4))
                dve.wait_ge(s["o"], nth("o", i, 2 * br + 2))
                for hh in range(2):
                    for j in range(2):
                        Sv = half(SS[br], hh)[:, :, j, 64 * hh:64 * hh + 64]
                        dve.wait_ge(*own(dve, i))
                        dve.tensor_tensor(Sv, Sv, half(dec, hh)[:, j, 1:9].unsqueeze(2).broadcast_to([64, DB, 64]),
                                          ALU.mult).then_inc(*give1(dve, "sdec"))
                return
            dve.wait_ge(s["o"], nth("o", i, 2 * br + c))
            if c == 1:
                dve.wait_ge(s["st"], nth("st", i, 8 * br + 4))
            for hh in range(2):
                for j in range(2):
                    v = slice(64 * hh, 64 * hh + 64)
                    dve.wait_ge(*own(dve, i))
                    dve.scalar_tensor_tensor(half(S[br][1 - c], hh)[:, j, v], half(S[br][c], hh)[:, j, v],
                                             half(dec, hh)[:, j, c:c + 1],
                                             half(M1, hh)[:, 128 * (2 * c + j) + 64 * hh:128 * (2 * c + j) + 64 * hh + 64],
                                             ALU.mult, ALU.add).then_inc(*give(dve, i, "st", 1))

        def gate(i, n, sg):
            first, T, NC, C = dims(i)
            dve.wait_ge(s["sg"], nth("sg", i, sg))
            dve.wait_ge(*own(dve, i))
            dve.tensor_tensor(X1[:, :, 0:T], X1[:, :, 0:T], X3[:, :, 0:T], ALU.mult).then_inc(*give(dve, i, "gz", 1))
            dve.wait_ge(s["gz"], nth("gz", i, n + 1))
            dve.wait_ge(*own(dve, i))
            dve.tensor_tensor(X4[:, :, 0:T], X4[:, :, 0:T], X1[:, :, 0:T], ALU.mult).then_inc(*give(dve, i, "mg", 1))

        def mix_lo(i, n):
            first, T, NC, C = dims(i)
            at = (2, 6, 0, 4)[n]
            dve.wait_ge(s["mhi"], nth("mhi", i, n + 1))
            dve.wait_ge(*own(dve, i))
            dve.tensor_tensor(m_lo[:, at:at + 2, 0:T], X4[:, :, 0:T], m_hi[:, at:at + 2, 0:T],
                              ALU.subtract).then_inc(*give(dve, i, "mlo", 1))

        def normalise(i, br):
            first, T, NC, C = dims(i)
            dve.wait_ge(s["nr"], nth("nr", i, br + 1))
            for j in range(2):
                dve.wait_ge(*own(dve, i))
                dve.scalar_tensor_tensor(X4[:, j, 0:T], M0[:, j * TT:j * TT + T], vec[:, V_GA + br, j:j + 1],
                                         X4[:, j, 0:T], ALU.mult, ALU.mult).then_inc(*give(dve, i, "on", 1))

        def convolution(i):
            first, T, NC, C = dims(i)
            dve.wait_ge(s["pj"], nth("pj", i, 10))
            dve.wait_ge(s["bc"], nth("bc", i, 1))
            if not first:
                dve.wait_ge(s["mlo"], nth("mlo", i, 0))
            L = LB0 if first else T + 2
            if first:
                dve.wait_ge(once["tcp"], 2)
                dve.wait_ge(*own(dve, i))
                dve.tensor_copy(seqs(X4, 18, DB, 2 + DS, 0, 2), TB[:, :, :, :]).then_inc(*give(dve, i, "hz", 1))
                P = pj[1][:, 0:2 * T].rearrange("p (j t) -> p j t", j=2)
                dve.wait_ge(*own(dve, i))
                dve.scalar_tensor_tensor(X4[:, :, 2:2 + META], P[:, :, 0:META], CS, X3[:, :, 0:META], ALU.mult,
                                         ALU.mult).then_inc(*give1(dve, "dd"))
                for j in range(2):
                    dve.wait_ge(*own(dve, i))
                    m = dve.scalar_tensor_tensor(seqs(X4, 18, DB, 2 + DS, 2, 2 + DS)[:, j],
                                             P[:, j, META:T0].rearrange("p (b w) -> p b w", w=DS), CS,
                                             X3[:, j, META:T0].rearrange("p (b w) -> p b w", w=DS), ALU.mult,
                                             ALU.mult)
                m.then_inc(*give(dve, i, "ub", 1))
            else:
                dve.wait_ge(*own(dve, i))
                dve.tensor_copy(X4[:, :, 0:2], tailB[:, :, :]).then_inc(*give(dve, i, "hz", 1))
                dve.wait_ge(*own(dve, i))
                dve.scalar_tensor_tensor(X4[:, :, 2:2 + T], pj[1][:, 0:2 * T].rearrange("p (j t) -> p j t", j=2), CS,
                                         X3[:, :, 0:T], ALU.mult, ALU.mult).then_inc(*give(dve, i, "ub", 1))
            dve.wait_ge(s["ub"], nth("ub", i, 1))
            dve.wait_ge(s["hz"], nth("hz", i, 1))
            for n in range(3):
                for j in range(2):
                    w = vec[:, V_CW + n, j:j + 1]
                    if n == 0:
                        dve.wait_ge(*own(dve, i))
                        dve.tensor_scalar(X3[:, j, 0:L - 2], X4[:, j, 0:L - 2], w, None, ALU.mult).then_inc(*give(dve, i, "cv", 1))
                    else:
                        dve.wait_ge(s["cv"], nth("cv", i, 2 * (n - 1) + j + 1))
                        dve.wait_ge(*own(dve, i))
                        dve.scalar_tensor_tensor(X3[:, j, 0:L - 2], X4[:, j, n:L - 2 + n], w, X3[:, j, 0:L - 2], ALU.mult,
                                                 ALU.add).then_inc(*give(dve, i, "cv", 1))
            dve.wait_ge(*own(dve, i))
            dve.tensor_copy(tailB[:, :, :], X4[:, :, META:META + 2] if first else X4[:, :, T:T + 2]).then_inc(*give(dve, i, "hz", 1))
            if first:
                dve.wait_ge(*own(dve, i))
                dve.tensor_copy(tl[:, :, 0:16].rearrange("p j (b w) -> p j b w", w=2), seqs(X4, 18, DB, 2 + DS, 4, 6)
                                ).then_inc(*give1(dve, "tl"))

        def conv_out(i):
            first, T, NC, C = dims(i)
            dve.wait_ge(s["pj"], nth("pj", i, 11))
            dve.wait_ge(s["cv"], nth("cv", i, 6))
            dve.wait_ge(s["hz"], nth("hz", i, 2))
            P = pj[0][:, 0:2 * T].rearrange("p (j t) -> p j t", j=2)
            if first:
                dve.wait_ge(once["tl"], 1)
                dve.wait_ge(*own(dve, i))
                dve.scalar_tensor_tensor(X4[:, :, 0:META], P[:, :, 0:META], CS, X3[:, :, 0:META], ALU.mult,
                                         ALU.mult).then_inc(*give1(dve, "dd"))
                for j in range(2):
                    dve.wait_ge(*own(dve, i))
                    m = dve.scalar_tensor_tensor(X4[:, j, META:T0].rearrange("p (b w) -> p b w", w=DS),
                                             P[:, j, META:T0].rearrange("p (b w) -> p b w", w=DS), CS,
                                             seqs(X3, 18, DB, 2 + DS, 0, DS)[:, j], ALU.mult, ALU.mult)
                m.then_inc(*give(dve, i, "bb", 1))
            else:
                dve.wait_ge(*own(dve, i))
                dve.scalar_tensor_tensor(X4[:, :, 0:T], P, CS, X3[:, :, 0:T], ALU.mult, ALU.mult).then_inc(*give(dve, i, "bb", 1))

        def pooling_in(i):
            first, T, NC, C = dims(i)
            dve.wait_ge(s["gz"], nth("gz", i, 1))
            if first:
                dve.wait_ge(*own(dve, i))
                dve.memset(X3[:, :, 0:POOLB], 0.0).then_inc(*give1(dve, "dd"))
                dve.memset(X3[:, :, POOLB + META:32], 0.0).then_inc(*give1(dve, "dd"))
                dve.wait_ge(*own(dve, i))
                dve.tensor_copy(seqs(X3, 32, DB, POOLB + DS, 0, POOLB), TD[:, :, :, :]).then_inc(*give(dve, i, "hz", 1))
            else:
                dve.wait_ge(*own(dve, i))
                dve.tensor_copy(X3[:, :, 0:POOLB], tailD[:, :, :]).then_inc(*give(dve, i, "hz", 1))

        def pooling(i):
            first, T, NC, C = dims(i)
            L = LD0 if first else T + POOLB
            dve.wait_ge(s["ud"], nth("ud", i, 1))
            dve.wait_ge(s["hz"], nth("hz", i, 3))
            dve.wait_ge(s["mlo"], nth("mlo", i, 1))
            dve.wait_ge(*own(dve, i))
            dve.tensor_tensor(X1[:, :, 1:L], X3[:, :, 1:L], X3[:, :, 0:L - 1], ALU.add).then_inc(*give(dve, i, "wn", 1))
            dve.wait_ge(s["wn"], nth("wn", i, 1))
            dve.wait_ge(*own(dve, i))
            dve.tensor_tensor(X4[:, :, 3:L], X1[:, :, 3:L], X1[:, :, 1:L - 2], ALU.add).then_inc(*give(dve, i, "wn", 1))
            dve.wait_ge(s["wn"], nth("wn", i, 2))
            dve.wait_ge(*own(dve, i))
            dve.tensor_tensor(X1[:, 1, 7:L], X4[:, 1, 7:L], X4[:, 1, 3:L - 4], ALU.add).then_inc(*give(dve, i, "wn", 1))
            dve.wait_ge(s["wn"], nth("wn", i, 3))
            dve.wait_ge(*own(dve, i))
            dve.tensor_tensor(X4[:, 1, 15:L], X1[:, 1, 15:L], X1[:, 1, 7:L - 8], ALU.add).then_inc(*give(dve, i, "wn", 1))
            dve.wait_ge(s["wn"], nth("wn", i, 4))
            for n, (hh, j, src, w) in enumerate(((0, 0, X1, 2), (1, 0, X4, 4), (0, 1, X1, 8), (1, 1, X4, 16))):
                out, win, u = half(X1, hh)[:, j, 15:L], half(src, hh)[:, j, 15:L], half(X3, hh)[:, j, 15:L]
                if first:
                    m = META + 1
                    dve.wait_ge(*own(dve, i))
                    dve.tensor_tensor(out[:, 0:m], win[:, 0:m], half(rcnt, hh)[:, j, :], ALU.mult).then_inc(*give1(dve, "pd0"))
                    dve.wait_ge(once["pd0"], n + 1)
                    dve.wait_ge(*own(dve, i))
                    dve.tensor_tensor(out[:, 0:m], out[:, 0:m], u[:, 0:m], ALU.subtract).then_inc(*give1(dve, "dd"))
                    dve.wait_ge(*own(dve, i))
                    dve.scalar_tensor_tensor(out[:, m:], win[:, m:], 1.0 / w, u[:, m:], ALU.mult,
                                             ALU.subtract).then_inc(*give(dve, i, "pd", 1))
                else:
                    dve.wait_ge(*own(dve, i))
                    dve.scalar_tensor_tensor(out, win, 1.0 / w, u, ALU.mult, ALU.subtract).then_inc(*give(dve, i, "pd", 1))
            dve.wait_ge(*own(dve, i))
            dve.tensor_copy(tailD[:, :, :], X3[:, :, META:META + POOLB] if first else X3[:, :, T:T + POOLB]
                            ).then_inc(*give(dve, i, "hz", 1))
            if first:
                for j in range(2):
                    dve.wait_ge(*own(dve, i))
                    m = dve.tensor_copy(tl[:, j, 16:48].rearrange("p (b w) -> p b w", w=DS),
                                    seqs(X3, 32, DB, POOLB + DS, POOLB, POOLB + DS)[:, j])
                m.then_inc(*give1(dve, "tl"))

        def x_scale(i, c):
            first, T, NC, C = dims(i)
            k = 2 // NC
            if c == 0:
                fresh("xn hlo")
            dve.wait_ge(s["rs"], nth("rs", i, k * (c + 1)))
            dve.wait_ge(*own(dve, i))
            dve.tensor_scalar(xbuf[0:C, :], xbuf[0:C, :], sx[0:C, c:c + 1], SH, ALU.mult, ALU.mult).then_inc(*give(dve, i, "xn", k))

        def x_lo(i, c):
            first, T, NC, C = dims(i)
            k = 2 // NC
            for n in range(2):
                dve.wait_ge(s["hhi"], nth("hhi", i, k * (2 * c + n + 1)))
                dve.wait_ge(*own(dve, i))
                dve.tensor_tensor(h_lo[:, 4 * n:4 * n + 4, c * CH:c * CH + C],
                                  op[:, 512 * n:512 * n + 512].rearrange("p (k t) -> p k t", k=4)[:, :, 0:C],
                                  h_hi[:, 4 * n:4 * n + 4, c * CH:c * CH + C], ALU.subtract).then_inc(*give(dve, i, "hlo", k))

        def w_out_lower():
            dve.wait_ge(once["sout"], 16 * 11)
            for u in range(2 * KD):
                n, k, at = u % len(wo_stage), u // 2, 512 * (u % 2)
                dve.wait_ge(once["wohi"], u + 1)
                dve.wait_ge(*own(dve, 0))
                dve.scalar_tensor_tensor(wo_lo[:, k, at:at + 512], wo_stage[n], SW, wo_hi[:, k, at:at + 512], ALU.mult,
                                         ALU.subtract).then_inc(*give1(dve, "wolo"))

        def dve_tile(i):
            begin(dve, i, 'la cf cq ub bb ab ls kcs qc bsc am qt st on hz cv wn pd od gz mg mlo', 'mlo')
            first, T, NC, C = dims(i)
            short = isinstance(i, int) and i == 1
            end = isinstance(i, int) and i == NT
            dve.wait_ge(s["pj"], nth("pj", i, 3))
            for j in range(2):
                dve.wait_ge(*own(dve, i))
                dve.tensor_scalar(X1[:, j, 0:T], pj[0][:, j * T:(j + 1) * T], vec[:, VB_A, j:j + 1], None,
                                  ALU.add).then_inc(*give(dve, i, "la", 1))
            dve.wait_ge(s["la"], nth("la", i, 2))
            if not first:
                dve.wait_ge(s["bsc"], nth("bsc", i, 0))
            absolute(i, 0, X1, X2)
            log_sigmoid(i, 0, X1, X2)
            running_sum(i, 0)
            if first:
                for u in range(len(stage), NU, 2):
                    lower(u)
            if short:
                w_out_lower()
            if not first:
                y_out(i - 1, 0)
            for lv in range(3):
                copy_scores(i, 0, lv)
            if not first and not short:
                y_out(i - 1, 1)
            copy_scores(i, 0, 3)
            dve.wait_ge(s["pj"], nth("pj", i, 7))
            dve.wait_ge(*own(dve, i))
            dve.tensor_scalar(X1[:, :, 0:T], pj[0][:, 0:2 * T].rearrange("p (j t) -> p j t", j=2), CS, None,
                              ALU.mult).then_inc(*give(dve, i, "cf", 1))
            dve.wait_ge(s["cf"], nth("cf", i, 1))
            dve.wait_ge(s["bsc"], nth("bsc", i, 1))
            absolute(i, 1, X1, X2)
            copy_scores(i, 0, 4)
            dve.wait_ge(s["pj"], nth("pj", i, 8))
            dve.wait_ge(*own(dve, i))
            dve.tensor_scalar(Q[1][:, :, 0:T], pj[1][:, 0:2 * T].rearrange("p (j t) -> p j t", j=2), CS, None,
                              ALU.mult).then_inc(*give(dve, i, "cq", 1))
            dve.wait_ge(s["cq"], nth("cq", i, 1))
            dve.wait_ge(s["lr"], nth("lr", i, 1))
            absolute(i, 2, Q[1], X3)
            log_sigmoid(i, 1, X1, X2)
            dve.wait_ge(s["ls"], nth("ls", i, 2))
            dve.wait_ge(*own(dve, i))
            dve.tensor_tensor(X1[:, :, 0:T], X2[:, :, 0:T], X1[:, :, 0:T], ALU.subtract).then_inc(*give(dve, i, "kcs", 1))
            log_sigmoid(i, 2, Q[1], X3)
            copy_scores(i, 0, 5)
            dve.wait_ge(s["sg"], nth("sg", i, 1))
            dve.wait_ge(*own(dve, i))
            dve.scalar_tensor_tensor(Q[1][:, :, 0:T], Q[1][:, :, 0:T], HK ** -0.5, X3[:, :, 0:T], ALU.mult,
                                     ALU.mult).then_inc(*give(dve, i, "qc", 1))
            copy_scores(i, 0, 6)
            convolution(i)
            copy_scores(i, 0, 7)
            query(i, 0)
            running_sum(i, 1)
            conv_out(i)
            dve.wait_ge(s["z"], nth("z", i, 1))
            absolute(i, 3, X1, X3)
            states(i, 0, 0)
            states(i, 0, 1)
            copy_scores(i, 1, 0)
            log_sigmoid(i, 3, X1, X3)
            copy_scores(i, 1, 1)
            gate(i, 0, 2)
            pooling_in(i)
            mix_lo(i, 0)
            copy_scores(i, 1, 2)
            pooling(i)
            copy_scores(i, 1, 3)
            copy_scores(i, 1, 4)
            dve.wait_ge(s["po"], nth("po", i, 1))
            for j in range(2):
                dve.wait_ge(*own(dve, i))
                dve.tensor_scalar(X4[:, j, 0:T], M1[:, j * TT:j * TT + T], vec[:, V_PS, j:j + 1], None,
                                  ALU.mult).then_inc(*give(dve, i, "od", 1))
            dve.wait_ge(s["z"], nth("z", i, 2))
            absolute(i, 4, X1, X3)
            copy_scores(i, 1, 5)
            log_sigmoid(i, 4, X1, X3)
            if not end:
                x_scale(i + 1, 0)
            copy_scores(i, 1, 6)
            gate(i, 1, 3)
            mix_lo(i, 1)
            if not end:
                x_lo(i + 1, 0)
            copy_scores(i, 1, 7)
            if not end:
                x_scale(i + 1, 1)
            normalise(i, 0)
            dve.wait_ge(s["z"], nth("z", i, 3))
            absolute(i, 5, X1, X3)
            query(i, 1)
            if not end:
                x_lo(i + 1, 1)
            log_sigmoid(i, 5, X1, X3)
            states(i, 1, 0)
            gate(i, 2, 4)
            mix_lo(i, 2)
            dve.wait_ge(s["z"], nth("z", i, 4))
            absolute(i, 6, X1, X3)
            states(i, 1, 1)
            log_sigmoid(i, 6, X1, X3)
            normalise(i, 1)
            gate(i, 3, 5)
            mix_lo(i, 3)

        def y_out(i, c):
            first, T, NC, C = dims(i)
            k = 2 // NC
            if c == 0:
                fresh("yg yo")
            dve.wait_ge(s["yr"], nth("yr", i, k * (c + 1)))
            dve.wait_ge(*own(dve, i))
            dve.scalar_tensor_tensor(op[0:C, :], op[0:C, :], sy[0:C, c:c + 1], gpost[0:C, :], ALU.mult,
                                     ALU.mult).then_inc(*give(dve, i, "yg", k))
            dve.wait_ge(s["yg"], nth("yg", i, k * (c + 1)))
            dve.wait_ge(s["xre"], nth("xre", i, 16 * k * (c + 1)))
            dve.wait_ge(*own(dve, i))
            dve.tensor_tensor(xbuf[0:C, :], op[0:C, :], xbuf[0:C, :], ALU.add).then_inc(*give(dve, i, "yo", k))

        sc_count = dve.alloc_register("sc_count")

        def own_values(b):
            V = (X1, X2)[b % 2][0:T0, :, :].rearrange("p j t -> p (j t)")[:, 0:2 * GW]
            dve.wait_ge(*own(dve, 0))
            dve.tensor_scalar(V, VI[0:T0, 0, :], seqm[:, b + 1:b + 2], None, ALU.mult).then_inc(*give1(dve, "vm"))

        def lower(u):
            times_norm(dve, u + 1, "wmud")
            for v in (u, u + 1):
                n, k = v // 2, 4 * (v % 2)
                dve.wait_ge(once["whi"], v + 1)
                dve.wait_ge(*own(dve, 0))
                dve.scalar_tensor_tensor(w_lo[:, k:k + 4, GW * n:GW * n + GW], stage[v % len(stage)], SW,
                                         w_hi[:, k:k + 4, GW * n:GW * n + GW], ALU.mult,
                                         ALU.subtract).then_inc(*give1(dve, "wlo"))

        @block.vector
        def _(_dve):
            i = 0
            dve.memset(cst[:, 0:1], EPS).then_inc(*give1(dve, "cstd"))
            dve.wait_ge(once["const0"], 16 * 3)
            dve.wait_ge(once["lrw"], 16)
            lr = B[:, 0, 0:KD * RANK].rearrange("p (k n) -> p k n", k=KD)
            dve.wait_ge(*own(dve, i))
            dve.tensor_tensor(lr, lr, gpre[:, :].unsqueeze(2).broadcast_to([128, KD, RANK]),
                              ALU.mult).then_inc(*give1(dve, "wlr"))
            dve.wait_ge(once["wlrh"], 1)
            dve.wait_ge(*own(dve, i))
            dve.scalar_tensor_tensor(w_lr[:, :, RANK:2 * RANK], lr, SW, w_lr[:, :, 0:RANK], ALU.mult,
                                     ALU.subtract).then_inc(*give1(dve, "wlr"))
            x_scale(0, 0)
            x_lo(0, 0)
            for u in range(0, len(stage), 2):
                lower(u)
            dve.wait_ge(once["const"], 16 * N_CONST)
            for dst, src in zip((masks[:, :], masks0[:, :], keep[:, :], keep0[:, :]), mask_f):
                dve.tensor_copy(dst, src).then_inc(*give1(dve, "msk"))
            dve.wait_ge(once["const0"], 16 * 3)
            dve.tensor_copy(eye[:, :], ident[:, :]).then_inc(*give1(dve, "msk"))
            dve.wait_ge(*own(dve, i))
            dve.tensor_scalar(gpost[:, :], gpost[:, :], OS, None, ALU.mult).then_inc(*give1(dve, "cstd"))
            dve.wait_ge(once["cstd"], 2)
            dve_tile(0)
            dve.wait_ge(once["sdec"], 8)
            for b in range(2):
                own_values(b)
            for b in range(DB):
                dve.wait_ge(once["su"], b + 1)
                for br in range(2):
                    for hh in range(2):
                        Sv = half(SS[br], hh)[:, b, :, 64 * hh:64 * hh + 64]
                        at = 512 * (b % 2) + 256 * br
                        dve.wait_ge(*own(dve, i))
                        dve.tensor_tensor(Sv, Sv, half(op, hh)[:, at:at + 256].rearrange(
                            "p (j v) -> p j v", j=2)[:, :, 64 * hh:64 * hh + 64], ALU.add).then_inc(*give1(dve, "sv"))
                if b + 2 < DB:
                    own_values(b + 2)
            dve.reg_mov(sc_count, SIGNALS["sc"])
            dve_tile(1)
            with dve.Fori(2, NT) as i:
                dve_tile(i)
            dve_tile(NT)
            y_out(NT, 0)
            y_out(NT, 1)


_INS = ("x_prompt", "x_sample", "state_gla", "state_conv", "state_hgrn", "state_pool", "meta_tokens", "norm_post", "w_in", "gla_w_a2", "pool_w", "w_out")
_OUTS = (("y_prompt", (SEQ, D), (1, SEQ, D)), ("y_sample", (DB, DS, D), (DB, DS, D)),
         ("gla_prompt", (4, HK, HK), (1, 1, 4, HK, HK)), ("conv_prompt", (2, GW), (1, 1, 2, GW)),
         ("hgrn_prompt", (4, HK, HK), (1, 1, 4, HK, HK)), ("pool_prompt", (POOLB, GW), (1, 1, POOLB, GW)),
         ("gla_sample", (DB, 4, HK, HK), (1, DB, 4, HK, HK)), ("conv_sample", (DB, 2, GW), (1, DB, 2, GW)),
         ("hgrn_sample", (DB, 4, HK, HK), (1, DB, 4, HK, HK)), ("pool_sample", (DB, POOLB, GW), (1, DB, POOLB, GW)))


def constants():
    import numpy as np
    p = np.arange(128)
    heads = (p[:, None] // HK == p[None, :] // HK)

    def level_mask(h, n, same):
        t = np.arange(n).reshape(-1, 2 * h)[:, h:].reshape(-1)
        q = np.arange(n)[:, None]
        return (q // (2 * h) == t // (2 * h)) & (q % (2 * h) < h) & same(q, t)

    masks = np.zeros((128, 8 * 64), np.float32)
    for lv, h in enumerate(LEVELS):
        masks[:, 64 * lv:64 * lv + 64] = level_mask(h, CH, lambda q, t: True)
    masks0 = np.zeros((T0, 4 * 24 + T0), np.float32)
    for n, h in enumerate(LEVELS[3:]):
        m = META if h >= 4 else T0
        masks0[:m, 24 * n:24 * n + m // 2] = level_mask(h, m, lambda q, t: True)
    masks0[:, 96:] = np.eye(T0)
    keep = np.ones((128, TT), np.float32)
    keep[:, ::CH] = 0
    keep0 = np.ones((128, T0), np.float32)
    keep0[:, 0] = 0
    keep0[:, META::DS] = 0
    rcnt = np.zeros((128, 2, META + 1), np.float32)
    for g, w in enumerate((2, 4, 8, 16)):
        r = rcnt[64 * (g % 2):64 * (g % 2) + 64, g // 2]
        r[:] = 1.0 / w
        r[:, :META] = (1.0 / np.minimum(np.arange(META) + 1, w)).astype(np.float32)
    seqm = np.zeros((T0, DB + 1), np.float32)
    seqm[:META, 0] = 1
    for b in range(DB):
        seqm[META + DS * b:META + DS * b + DS, b + 1] = 1
    return dict(c_ident=np.eye(128, dtype=np.float32), c_bones=heads.astype(np.float32), c_masks=masks,
                c_masks0=masks0, c_keep=keep, c_keep0=keep0,
                c_rcnt=rcnt, c_seqm=seqm)


def kernel(**inputs):
    import numpy as np
    import concourse.bacc as bacc
    from concourse.bass_utils import run_bass_kernel_spmd

    nc = bacc.Bacc("TRN2", target_bir_lowering=False, num_devices=1)
    arrays, aps = {}, {}

    def add(name, x):
        arrays["in_" + name] = x
        aps[name] = nc.dram_tensor("in_" + name, x.shape, mybir.dt.from_np(x.dtype), kind="ExternalInput").ap()

    for name in _INS:
        x = np.ascontiguousarray(inputs[name])
        if name not in ("x_sample", "meta_tokens"):
            x = x[0]
        add(name, x)
    add("norm_pre", np.ascontiguousarray(np.asarray(inputs["norm_pre"])[0].reshape(KD, 128).T))
    rows = [np.asarray(inputs[name])[0].reshape(-1, GW)
            for name in ("gla_b_a", "gla_norm", "hgrn_norm", "pool_scale", "conv_w")]
    add("vectors", np.ascontiguousarray(np.concatenate(rows).reshape(7, 2, 128).transpose(2, 0, 1)))
    for name, x in constants().items():
        add(name, x)
    outs = {name: nc.dram_tensor("out_" + name, shape, F32, kind="ExternalOutput").ap() for name, shape, _ in _OUTS}
    program(nc, aps, outs)
    r = run_bass_kernel_spmd(nc, [arrays], core_ids=[0]).results[0]
    return tuple(r["out_" + name].reshape(full) for name, _, full in _OUTS)
```
